# Optimizing a Trainium2 kernel written in Bass

```python
import jax, jax.numpy as jnp
from jax import lax
import numpy as np

D_MODEL = 1024
BATCH = 1
SEQ = 1024
DEPTH = 1
DEC_BATCH = 1
DEC_SEQ = 256
PAST_LEN = 128

GRID_W = 64
WIN_H = 8
WIN_W = 16
NA_HEADS = 8
NA_HEAD_DIM = 64
D_NA = NA_HEADS * NA_HEAD_DIM
RWKV_HEADS = 8
RWKV_HEAD_DIM = 64
D_RWKV = RWKV_HEADS * RWKV_HEAD_DIM
DECAY_LORA = 64
ICLR_LORA = 64
GATE_LORA = 128
N_DIR = 2
D_FF = 4 * D_MODEL
N_BRANCH = 2
D_SHIFT = 3 * D_RWKV + N_DIR * DECAY_LORA + N_DIR * ICLR_LORA + GATE_LORA
D_IN = 3 * D_NA + D_SHIFT + N_BRANCH * D_MODEL
RMS_EPS = 1e-6
GN_EPS = 64e-5

kernel_name = 'hybrid_natten_rwkv7_encoder'

def rmsnorm(x, g):
    xf = x.astype(jnp.float32)
    y = xf * lax.rsqrt(jnp.mean(xf * xf, axis=-1, keepdims=True) + RMS_EPS)
    return (y * g.astype(jnp.float32)).astype(x.dtype)

def neighbourhood_attention(q, k, v, rpb):
    b, L, _ = q.shape
    rows = L // GRID_W
    kh = min(WIN_H, rows)
    shp = (b, rows, GRID_W, NA_HEADS, NA_HEAD_DIM)
    qg = q.reshape(shp) * (NA_HEAD_DIM ** -0.5)
    kg = k.reshape(shp)
    vg = v.reshape(shp)
    r = jnp.arange(rows)
    row_start = jnp.clip(r - kh // 2, 0, rows - kh)
    key_rows = row_start[:, None] + jnp.arange(kh)[None, :]
    k_blk = kg[:, key_rows]
    v_blk = vg[:, key_rows]
    s = jnp.einsum('brqhd,brkwhd->bhrqkw', qg, k_blk).astype(jnp.float32)
    c = jnp.arange(GRID_W)
    col_start = jnp.clip(c - WIN_W // 2, 0, GRID_W - WIN_W)
    col_ok = (c[None, :] >= col_start[:, None]) & (c[None, :] < col_start[:, None] + WIN_W)
    row_idx = key_rows - r[:, None] + (WIN_H - 1)
    col_idx = jnp.clip(c[None, :] - c[:, None] + (WIN_W - 1), 0, 2 * WIN_W - 2)
    bias = rpb[:, row_idx[:, None, :, None], col_idx[None, :, None, :]]
    s = s + bias[None].astype(jnp.float32)
    s = jnp.where(col_ok[:, None, :], s, -jnp.inf)
    p = jax.nn.softmax(s.reshape(b, NA_HEADS, rows, GRID_W, kh * GRID_W), axis=-1)
    p = p.reshape(s.shape).astype(v.dtype)
    o = jnp.einsum('bhrqkw,brkwhd->brqhd', p, v_blk)
    return o.reshape(b, L, D_NA)

def centred_shift(p, mu_prev, mu_next):
    prev = jnp.pad(p[:, :-1], ((0, 0), (1, 0), (0, 0)))
    nxt = jnp.pad(p[:, 1:], ((0, 0), (0, 1), (0, 0)))
    return p + mu_prev * (prev - p) + mu_next * (nxt - p)

def rwkv7_scan(r, w, k, v, a, bb):
    b, L, nd, H, N = r.shape

    def step(S, inp):
        r_t, w_t, k_t, v_t, a_t, b_t = inp
        sa = jnp.einsum('zdhij,zdhj->zdhi', S, a_t)
        S = S * w_t[..., None, :] + sa[..., :, None] * b_t[..., None, :] + v_t[..., :, None] * k_t[..., None, :]
        y = jnp.einsum('zdhij,zdhj->zdhi', S, r_t)
        return S, y

    xs = (jnp.moveaxis(r, 1, 0), jnp.moveaxis(w, 1, 0), jnp.moveaxis(k, 1, 0),
          jnp.moveaxis(v, 1, 0), jnp.moveaxis(a, 1, 0), jnp.moveaxis(bb, 1, 0))
    S0 = jnp.zeros((b, nd, H, N, N), jnp.float32)
    _, y = lax.scan(step, S0, xs)
    return jnp.moveaxis(y, 0, 1)

def rwkv7_mixer(p, w0, w2, a0, a2, g2, k_k, k_a, r_k, ln_w, ln_b):
    b, L, _ = p.shape
    H, N = RWKV_HEADS, RWKV_HEAD_DIM
    f32 = jnp.float32
    r = p[..., 0:D_RWKV]
    k = p[..., D_RWKV:2 * D_RWKV]
    v = p[..., 2 * D_RWKV:3 * D_RWKV]
    off = 3 * D_RWKV
    wl = p[..., off:off + N_DIR * DECAY_LORA].reshape(b, L, N_DIR, DECAY_LORA)
    off = off + N_DIR * DECAY_LORA
    al = p[..., off:off + N_DIR * ICLR_LORA].reshape(b, L, N_DIR, ICLR_LORA)
    off = off + N_DIR * ICLR_LORA
    gl = p[..., off:off + GATE_LORA]
    w_log = -jax.nn.softplus(-(w0 + jnp.einsum('bldr,drc->bldc', jnp.tanh(wl), w2))) - 0.5
    decay = jnp.exp(-jnp.exp(w_log.astype(f32)))
    iclr = jax.nn.sigmoid((a0 + jnp.einsum('bldr,drc->bldc', al, a2)).astype(f32))
    g = jax.nn.sigmoid(gl) @ g2
    kk = (k * k_k).astype(f32).reshape(b, L, 1, H, N)
    kk = kk * lax.rsqrt(jnp.sum(kk * kk, axis=-1, keepdims=True) + 1e-12)
    k_dir = (k[:, :, None].astype(f32) * (1.0 + (iclr - 1.0) * k_a.astype(f32))).reshape(b, L, N_DIR, H, N)
    iclr_h = iclr.reshape(b, L, N_DIR, H, N)
    r_h = r.astype(f32).reshape(b, L, 1, H, N)
    v_h = v.astype(f32).reshape(b, L, 1, H, N)

    def both(t):
        t = jnp.broadcast_to(t.astype(f32), (b, L, N_DIR, H, N))
        return jnp.stack([t[:, :, 0], jnp.flip(t[:, :, 1], axis=1)], axis=2)

    y = rwkv7_scan(both(r_h), both(decay.reshape(b, L, N_DIR, H, N)), both(k_dir),
                   both(v_h), both(-kk), both(kk * iclr_h))
    y = y[:, :, 0] + jnp.flip(y[:, :, 1], axis=1)
    mean = jnp.mean(y, axis=-1, keepdims=True)
    var = jnp.mean(jnp.square(y - mean), axis=-1, keepdims=True)
    y = (y - mean) * lax.rsqrt(var + GN_EPS) * ln_w.astype(f32).reshape(H, N) + ln_b.astype(f32).reshape(H, N)
    bonus = jnp.sum(r_h * k_dir * r_k.astype(f32), axis=(2, 4))[..., None] * v_h[:, :, 0]
    out = (y + bonus).reshape(b, L, D_RWKV).astype(p.dtype)
    return out * g

def encoder_layer(x, w_in, b_gate, rpb, mu_prev, mu_next, w0, w2, a0, a2, g2, k_k, k_a, r_k,
                  ln_w, ln_b, w_proj_a, w_proj_b, w_out, w_up, w_down,
                  norm_pre_mix, norm_post_mix, norm_pre_ffn, norm_post_ffn):
    h = rmsnorm(x, norm_pre_mix)
    proj = jnp.einsum('bld,de->ble', h, w_in)
    q_na = proj[..., 0:D_NA]
    k_na = proj[..., D_NA:2 * D_NA]
    v_na = proj[..., 2 * D_NA:3 * D_NA]
    o_na = neighbourhood_attention(q_na, k_na, v_na, rpb)
    shifted = centred_shift(proj[..., 3 * D_NA:3 * D_NA + D_SHIFT], mu_prev, mu_next)
    o_rw = rwkv7_mixer(shifted, w0, w2, a0, a2, g2, k_k, k_a, r_k, ln_w, ln_b)
    gates = jax.nn.sigmoid(proj[..., 3 * D_NA + D_SHIFT:] + b_gate)
    merged = gates[..., :D_MODEL] * (o_na @ w_proj_a) + gates[..., D_MODEL:] * (o_rw @ w_proj_b)
    x = x + rmsnorm(merged @ w_out, norm_post_mix)
    h = rmsnorm(x, norm_pre_ffn)
    f = jnp.square(jax.nn.relu(h @ w_up)) @ w_down
    return x + rmsnorm(f, norm_post_ffn)

def trunk(x, layer_params):
    for i in range(DEPTH):
        x = encoder_layer(x, *[prm[i] for prm in layer_params])
    return x

def setup_inputs(seed: int = 0) -> dict:
    key = jax.random.key(seed)
    ks = jax.random.split(key, 32)
    f32 = jnp.float32

    def nrm(k, shape, scale):
        return jax.random.normal(k, shape, f32) * scale

    return {
        'x_prompt': nrm(ks[0], (BATCH, SEQ, D_MODEL), 1.0),
        'x_sample': nrm(ks[1], (DEC_BATCH, DEC_SEQ, D_MODEL), 1.0),
        'w_in': nrm(ks[2], (DEPTH, D_MODEL, D_IN), D_MODEL ** -0.5),
        'b_gate': nrm(ks[3], (DEPTH, N_BRANCH * D_MODEL), 0.1),
        'rpb': nrm(ks[4], (DEPTH, NA_HEADS, 2 * WIN_H - 1, 2 * WIN_W - 1), 0.1),
        'mu_prev': jax.random.uniform(ks[5], (DEPTH, D_SHIFT), f32, 0.0, 0.5),
        'mu_next': jax.random.uniform(ks[6], (DEPTH, D_SHIFT), f32, 0.0, 0.5),
        'w0': jax.random.uniform(ks[7], (DEPTH, N_DIR, D_RWKV), f32, -6.0, -0.5),
        'w2': nrm(ks[8], (DEPTH, N_DIR, DECAY_LORA, D_RWKV), 0.1),
        'a0': nrm(ks[9], (DEPTH, N_DIR, D_RWKV), 0.1),
        'a2': nrm(ks[10], (DEPTH, N_DIR, ICLR_LORA, D_RWKV), 0.1),
        'g2': nrm(ks[11], (DEPTH, GATE_LORA, D_RWKV), GATE_LORA ** -0.5),
        'k_k': 0.85 + nrm(ks[12], (DEPTH, D_RWKV), 0.02),
        'k_a': 1.0 + nrm(ks[13], (DEPTH, D_RWKV), 0.02),
        'r_k': nrm(ks[14], (DEPTH, RWKV_HEADS, RWKV_HEAD_DIM), 0.1),
        'ln_w': 1.0 + nrm(ks[15], (DEPTH, D_RWKV), 0.02),
        'ln_b': nrm(ks[16], (DEPTH, D_RWKV), 0.02),
        'w_proj_a': nrm(ks[17], (DEPTH, D_NA, D_MODEL), D_NA ** -0.5),
        'w_proj_b': nrm(ks[18], (DEPTH, D_RWKV, D_MODEL), D_RWKV ** -0.5),
        'w_out': nrm(ks[19], (DEPTH, D_MODEL, D_MODEL), D_MODEL ** -0.5),
        'w_up': nrm(ks[20], (DEPTH, D_MODEL, D_FF), D_MODEL ** -0.5),
        'w_down': nrm(ks[21], (DEPTH, D_FF, D_MODEL), D_FF ** -0.5),
        'norm_pre_mix': 1.0 + nrm(ks[22], (DEPTH, D_MODEL), 0.02),
        'norm_post_mix': 1.0 + nrm(ks[23], (DEPTH, D_MODEL), 0.02),
        'norm_pre_ffn': 1.0 + nrm(ks[24], (DEPTH, D_MODEL), 0.02),
        'norm_post_ffn': 1.0 + nrm(ks[25], (DEPTH, D_MODEL), 0.02),
    }

def reference(x_prompt, x_sample, w_in, b_gate, rpb, mu_prev, mu_next, w0, w2, a0, a2, g2,
              k_k, k_a, r_k, ln_w, ln_b, w_proj_a, w_proj_b, w_out, w_up, w_down,
              norm_pre_mix, norm_post_mix, norm_pre_ffn, norm_post_ffn):
    layer_params = (w_in, b_gate, rpb, mu_prev, mu_next, w0, w2, a0, a2, g2, k_k, k_a, r_k,
                    ln_w, ln_b, w_proj_a, w_proj_b, w_out, w_up, w_down,
                    norm_pre_mix, norm_post_mix, norm_pre_ffn, norm_post_ffn)
    y_prompt = trunk(x_prompt, layer_params)
    y_sample = trunk(x_sample, layer_params)
    return (y_prompt, y_sample)


_drawn_inputs = setup_inputs


def setup_inputs(seed=0):
    import zlib

    import numpy as np

    out = dict(_drawn_inputs(seed))
    spreads = {}
    factors = {'k_k': 10.674,
     'k_a': 3.349,
     'ln_w': 11.079,
     'ln_b': 12.224,
     'norm_post_mix': 10.631,
     'norm_pre_ffn': 39.087,
     'norm_post_ffn': 58.468,
     'rpb': 6.24}
    for name, (base, spread) in spreads.items():
        noise = np.random.default_rng([zlib.crc32(name.encode()), seed]).standard_normal(out[name].shape)
        drawn = base * np.exp(spread * noise) if base else spread * noise
        out[name] = __import__('jax').numpy.asarray(drawn.astype(out[name].dtype))
    for name, factor in factors.items():
        out[name] = (out[name] * factor).astype(out[name].dtype)
    return out
```

```python
import concourse.bass as bass
from concourse import mybir
from contextlib import ExitStack

F32 = mybir.dt.float32
ACT = mybir.ActivationFunctionType
ALU = mybir.AluOpType
AX = mybir.AxisListType

P = 128
D = 1024
KD = D // P
TP, TS = 1024, 256
T = TP + TS
NT = T // P
GROUPS = ((0, 512), (512, 512), (1024, 256))
NG = len(GROUPS)
GRID_W = 64
WIN_H, WIN_W = 8, 16
HD = 64
CT = 4
D_SH = 1920
E_SH = D_SH // P
DFF = 4096
FG = 4
FT = DFF // P // FG
C = 64
NC = T // C
NC_P = TP // C
LEVELS = 5
DECAY = -0.6065306597126334
RMS_EPS, GN_EPS, KK_EPS = 1e-6, 64e-5, 1e-12
NEG = -1e30

PM_MUP, PM_MUN, PM_G1, PM_G2 = 0, 15, 30, 38
PM_RK = 46
NPC = 9
PM_EPS = PM_RK + CT * NPC
PM_N = PM_EPS + 3
(W0A, W0B, A0A, A0B, K_K, K_A, R_K, LN_W, LN_B, K_1A) = range(10)

CN_ID, CN_ONES, CN_MEAN = 0, 128, 256
CN_N = 384
CS_G = T + 2 * NC
CS_F = CS_G + 2 * 4 * P
CS_L = CS_F + 2 * P
CS_N = CS_L + 2 * LEVELS * P

E_B0 = 12
E_WL, E_AL, E_GL = 12, 13, 14


def bcast(ap, n):
    return ap.to_broadcast([ap.shape[0], n])


class Steps:

    def __init__(self, eng, sem, base=0):
        self.eng, self.sem, self.base, self.n = eng, sem, base, 0

    def mark(self, ins):
        self.n += 1
        ins.then_inc(self.sem, 1)

    def wait(self):
        self.eng.wait_ge(self.sem, self.base + self.n)


def norm_to_channels(nc, x, params, ident, hT):
    with ExitStack() as ctx:
        sb = lambda n, s: ctx.enter_context(nc.sbuf_tensor(n, s, F32))
        sem = lambda n: ctx.enter_context(nc.semaphore(n))
        xs = [sb(f"n1_x{j}", [P, D]) for j in range(2)]
        xn = [sb(f"n1_xn{j}", [P, D]) for j in range(2)]
        sq = sb("n1_sq", [P, D])
        st = [sb(f"n1_st{j}", [P, 3]) for j in range(2)]
        ps = [ctx.enter_context(nc.psum_tensor(f"n1_ps{j}", [P, D], F32)) for j in range(2)]
        x_in = [sem(f"n1_x_in{j}") for j in range(2)]
        sq_done, rms_ready, rstd_ready = sem("n1_sq_done"), sem("n1_rms"), sem("n1_rstd")
        xn_ready, tr_ready, h_ready = sem("n1_xn"), sem("n1_tr"), sem("n1_h")
        block = ctx.enter_context(nc.Block())
        xr = x.rearrange("(n p) d -> n p d", p=P)

        @block.sync
        def _(sp):
            with sp.Fori(0, NT // 2) as i:
                for j in range(2):
                    n = i * 2 + j
                    sp.wait_ge(xn_ready, n + 1)
                    sp.dma_start(xs[j][:, :], xr[n, :, :]).then_inc(x_in[j], 16)

        @block.scalar
        def _(act):
            with act.Fori(0, NT // 2) as i:
                for j in range(2):
                    n = i * 2 + j
                    act.wait_ge(x_in[j], i * 16 + 16)
                    nc.scalar.activation(sq[:, :], xs[j][:, :], ACT.Square,
                                         accum_out=st[j][:, 0:1]).then_inc(sq_done, 1)
                    act.wait_ge(sq_done, n + 1)
                    nc.scalar.activation(st[j][:, 1:2], st[j][:, 0:1], ACT.Sqrt, scale=1.0 / D,
                                         bias=params[:, PM_EPS:PM_EPS + 1]).then_inc(rms_ready, 1)

        @block.vector
        def _(dve):
            dve.sem_inc(xn_ready, 2)
            dve.sem_inc(h_ready, 2)
            with dve.Fori(0, NT // 2) as i:
                for j in range(2):
                    n = i * 2 + j
                    dve.wait_ge(rms_ready, n + 1)
                    nc.vector.reciprocal(st[j][:, 2:3], st[j][:, 1:2]).then_inc(rstd_ready, 1)
                    dve.wait_ge(rstd_ready, n + 1)
                    dve.wait_ge(tr_ready, n + 1)
                    nc.vector.tensor_scalar(xn[j][:, :], xs[j][:, :], st[j][:, 2:3], None,
                                            ALU.mult).then_inc(xn_ready, 1)
                    dve.wait_ge(tr_ready, n + 3)
                    nc.vector.tensor_tensor(
                        hT[:, :, bass.ts(n, P)], ps[j][:, :].rearrange("p (k t) -> p k t", k=KD),
                        params[:, PM_G1:PM_G1 + KD].unsqueeze(2).to_broadcast([P, KD, P]),
                        ALU.mult).then_inc(h_ready, 1)

        @block.tensor
        def _(pe):
            pe.sem_inc(tr_ready, 2)
            with pe.Fori(0, NT // 2) as i:
                for j in range(2):
                    n = i * 2 + j
                    pe.wait_ge(xn_ready, n + 3)
                    pe.wait_ge(h_ready, n + 1)
                    for k in range(KD):
                        last = nc.tensor.transpose(ps[j][:, k * P:(k + 1) * P],
                                                   xn[j][:, k * P:(k + 1) * P], ident)
                    last.then_inc(tr_ready, 1)


def shifted_projection(nc, w_in, params, hT, hT_dram, sT):
    with ExitStack() as ctx:
        sb = lambda n, s: ctx.enter_context(nc.sbuf_tensor(n, s, F32))
        sem = lambda n: ctx.enter_context(nc.semaphore(n))
        w = [sb(f"sp_w{j}", [P, D]) for j in range(2)]
        raw = [sb(f"sp_raw{j}", [P, T]) for j in range(2)]
        acc = [sb(f"sp_acc{j}", [P, T]) for j in range(2)]
        c0 = sb("sp_c0", [P, E_SH])
        ps = [ctx.enter_context(nc.psum_tensor(f"sp_ps{j}", [P, 1536], F32)) for j in range(2)]
        w_ld = [sem(f"sp_w_ld{j}") for j in range(2)]
        gemm, raw_ready, shifted, own_scaled, prev_added = (
            sem("sp_gemm"), sem("sp_raw"), sem("sp_shifted"), sem("sp_own"), sem("sp_prev"))
        c0_ready, h_out, lora_done = sem("sp_c0"), sem("sp_h_out"), sem("sp_lora")
        block = ctx.enter_context(nc.Block())

        def tiles(eng, body):
            with eng.Fori(0, E_SH // 2) as i:
                for j in range(2):
                    body(i * 2 + j, j, i)
            body(E_SH - 1, 0, E_SH // 2)

        @block.sync
        def _(sp):
            sp.dma_start(hT_dram, hT.rearrange("p k t -> p (k t)")).then_inc(h_out, 16)

            def load(e, j, turn):
                sp.wait_ge(gemm, e * NG + NG)
                sp.dma_start(w[j][:, :], w_in[e + E_B0, :, :]).then_inc(w_ld[j], 16)
            tiles(sp, load)
            sp.wait_ge(h_out, 16)

        @block.tensor
        def _(pe):
            pe.sem_inc(gemm, 2 * NG)

            def gemms(e, j, turn):
                pe.wait_ge(w_ld[j], turn * 16 + 16)
                for g, (t0, tn) in enumerate(GROUPS):
                    pe.wait_ge(raw_ready, e * NG + (g + 1))
                    for k in range(KD):
                        last = nc.tensor.matmul(ps[j][:, t0:t0 + tn], w[j][:, k * P:(k + 1) * P],
                                                hT[:, k, t0:t0 + tn], start=k == 0, stop=k == KD - 1)
                    last.then_inc(gemm, 1)
            tiles(pe, gemms)

        @block.scalar
        def _(act):
            act.sem_inc(raw_ready, 2 * NG)

            def evacuate(e, j, turn):
                act.wait_ge(shifted, e + 1)
                for g, (t0, tn) in enumerate(GROUPS):
                    act.wait_ge(gemm, e * NG + (2 * NG + g + 1))
                    nc.scalar.activation(raw[j][:, t0:t0 + tn], ps[j][:, t0:t0 + tn],
                                         ACT.Copy).then_inc(raw_ready, 1)
            tiles(act, evacuate)
            act.wait_ge(shifted, E_SH + 2)
            nc.scalar.activation(sT[:, E_WL, :], sT[:, E_WL, :], ACT.Tanh).then_inc(lora_done, 1)
            nc.scalar.activation(sT[:, E_GL, :], sT[:, E_GL, :], ACT.Sigmoid).then_inc(lora_done, 1)

        @block.vector
        def _(dve):
            dve.sem_inc(shifted, 2)
            nc.vector.tensor_tensor(c0[:, :], params[:, PM_MUP:PM_MUP + E_SH],
                                    params[:, PM_MUN:PM_MUN + E_SH], ALU.add).then_inc(c0_ready, 1)
            dve.wait_ge(c0_ready, 1)
            nc.vector.tensor_scalar(c0[:, :], c0[:, :], -1.0, 1.0, ALU.mult, ALU.add).then_inc(c0_ready, 1)
            dve.wait_ge(c0_ready, 2)

            def shift(e, j, turn):
                dve.wait_ge(raw_ready, e * NG + 3 * NG)
                nc.vector.tensor_scalar(acc[j][:, :], raw[j][:, :], c0[:, bass.ds(e, 1)], None,
                                        ALU.mult).then_inc(own_scaled, 1)
                dve.wait_ge(own_scaled, e + 1)
                for lo, hi in ((1, TP), (TP + 1, T)):
                    nc.vector.scalar_tensor_tensor(
                        acc[j][:, lo:hi], raw[j][:, lo - 1:hi - 1],
                        params[:, bass.ds(e + PM_MUP, 1)], acc[j][:, lo:hi],
                        ALU.mult, ALU.add).then_inc(prev_added, 1)
                dve.wait_ge(prev_added, e * 2 + 2)
                for lo, hi in ((0, TP - 1), (TP, T - 1)):
                    nc.vector.scalar_tensor_tensor(
                        sT[:, bass.ds(e, 1), lo:hi], raw[j][:, lo + 1:hi + 1],
                        params[:, bass.ds(e + PM_MUN, 1)], acc[j][:, lo:hi], ALU.mult, ALU.add)
                nc.vector.tensor_copy(sT[:, bass.ds(e, 1), TP - 1:T:TS], acc[j][:, TP - 1:T:TS]
                                      ).then_inc(shifted, 1)
            tiles(dve, shift)
            dve.wait_ge(shifted, E_SH + 2)


def scan_mixer(nc, lora, params, cn_scan, ident, ones, mean, ab, sT):
    with ExitStack() as ctx:
        sb = lambda n, s: ctx.enter_context(nc.sbuf_tensor(n, s, F32))
        sems = []

        def sem(n):
            sems.append(nc.alloc_semaphore("sc_" + n))
            return sems[-1]

        AR = ab[:, 0:9 * T].rearrange("p (n t) -> p n t", t=T)
        AX_ = [dict(a=0, r=1, b=2, k=3), dict(k=5, b=6, r=7, a=8)]
        V = 4
        kk, lw, cum, neg, icl, kds = (ab[:, (9 + n) * T:(10 + n) * T] for n in range(6))
        y = [lw, cum]
        wl = sb("sc_lora", [P, 3, P])
        pc = sb("sc_pc", [P, NPC + 1])
        edge = sb("sc_edge", [P, 2, NC])
        cs = sb("sc_cs", [P, CS_N])
        reset, keep = cs[:, 0:T], cs[:, T:T + 2 * NC].rearrange("p (d c) -> p d c", d=2)
        gmask = [cs[:, CS_G + d * 4 * P:CS_G + (d + 1) * 4 * P] for d in range(2)]
        first = [cs[:, CS_F + d * P:CS_F + (d + 1) * P] for d in range(2)]
        lmask = [cs[:, CS_L + d * LEVELS * P:CS_L + (d + 1) * LEVELS * P]
                 .rearrange("p (l t) -> p l t", l=LEVELS) for d in range(2)]
        BD = [sb(f"sc_bd{d}", [P, 6, P]) for d in range(2)]
        BX = [dict(a=1, r=2, b=3, k=4, v=5), dict(v=1, k=2, b=3, r=4, a=5)]
        WK = [sb(f"sc_wk{d}", [P, 13, P]) for d in range(2)]
        GX = [dict(ab=5, rb=6, ak=7, rk=8), dict(rb=5, ab=6, rk=7, ak=8)]
        ML = [sb(f"sc_ml{d}", [P, LEVELS, P]) for d in range(2)]
        XY = [sb(f"sc_xy{d}", [P, 2, P]) for d in range(2)]
        Q1 = [sb(f"sc_q{d}", [P, P]) for d in range(2)]
        S = [sb(f"sc_s{d}", [P, P]) for d in range(2)]
        ps = ctx.enter_context(nc.psum_tensor("sc_ps", [P, 8, 512], F32))
        psA = ps[:, 0:3, :].rearrange("p b n -> p (b n)")
        psB = ps[:, 4:7, :].rearrange("p b n -> p (b n)")

        cs_in, zeroed, lora_in = sem("cs_in"), sem("zeroed"), sem("lora_in")
        pc_ready, sq_ready, ss_ps, nrm_ready, kk_ready = (
            sem("pc"), sem("sq"), sem("ss_ps"), sem("nrm"), sem("kk"))
        zw_ps, za_ps, sg_ready, icl_ready, cum_ready, exps_ready, arr_ready = (
            sem("zw_ps"), sem("za_ps"), sem("sg"), sem("icl"), sem("cum"), sem("exps"), sem("arr"))
        dch, pdone = sem("dch"), sem("pair_done")
        ysum, mean_ps, yc_ready, ysq, var_ps, std_ready, bq_ready, gb_ps = (
            sem("ysum"), sem("mean_ps"), sem("yc"), sem("ysq"), sem("var_ps"), sem("std"),
            sem("bq"), sem("gb_ps"))
        two = lambda n: [sem(f"{n}{d}") for d in range(2)]
        bd_ready, gram, bytok, masked, copied = (
            two("bd"), two("gram"), two("bytok"), two("masked"), two("copied"))
        bd_ready2 = two("bd2_")
        lvl_ready, y1_ready, x1t, x1c = two("lvl"), two("y1"), two("x1t"), two("x1c")
        q_ps, q_ready, xy_ps, xy_ready = two("q_ps"), two("q"), two("xy_ps"), two("xy")
        w1_ps, w1_ready, u_ps, u_ready = two("w1_ps"), two("w1"), two("u_ps"), two("u")
        m_ps, m_ready, s_ps, s_ready, y_ready, y1h = (
            two("m_ps"), two("m"), two("s_ps"), two("s"), two("y"), two("y1h"))
        NDCH = 15
        block = ctx.enter_context(nc.Block())

        def chunk_of(d, j):
            return j if d == 0 else j * -1 + (NC - 1)

        @block.sync
        def _(sp):
            sp.dma_start(cs[:, :], cn_scan).then_inc(cs_in, 16)
            with sp.Fori(0, CT) as ct:
                sp.wait_ge(pdone, ct + 1)
                sp.dma_start(wl[:, :, :], lora[ct, :, :, :]).then_inc(lora_in, 16)

        @block.gpsimd
        def _(pool):
            for d in range(2):
                nc.gpsimd.memset(BD[d][:, 1:6, :], 0.0).then_inc(zeroed, 1)
                nc.gpsimd.tensor_copy(BD[d][:, 0, :], ident).then_inc(zeroed, 1)
                nc.gpsimd.memset(S[d][:, :], 0.0).then_inc(zeroed, 1)
            pool.wait_ge(zeroed, 6)
            pool.wait_ge(cs_in, 16)
            with pool.Fori(0, CT) as ct:
                with pool.Fori(0, NC) as j:
                    q = ct * NC + j
                    pool.wait_ge(arr_ready, ct * 2 + 2)
                    for d in range(2):
                        pool.wait_ge(m_ready[d], q + 1)
                        nc.gpsimd.tensor_copy(BD[d][C:P, 1:6, C:P],
                                              AR[C:P, 4 * d:4 * d + 5, bass.ts(chunk_of(d, j), C)]
                                              ).then_inc(bd_ready2[d], 1)
                    pool.wait_ge(bd_ready2[1], q + 1)
                    for d in range(2):
                        pool.wait_ge(masked[d], q + 1)
                        nc.gpsimd.tensor_tensor(
                            ML[d][:, :, :],
                            WK[d][:, GX[d]["ab"], :].unsqueeze(1).to_broadcast([P, LEVELS, P]),
                            lmask[d], ALU.mult).then_inc(lvl_ready[d], 1)

        @block.tensor
        def _(pe):
            def over_tokens(dst, lhsT, rhs):
                for t0, tn in GROUPS:
                    last = nc.tensor.matmul(dst[:, t0:t0 + tn], lhsT, rhs[:, t0:t0 + tn],
                                            start=True, stop=True)
                return last

            pe.wait_ge(zeroed, 6)
            with pe.Fori(0, CT) as ct:
                pe.wait_ge(lora_in, ct * 16 + 16)
                pe.wait_ge(sq_ready, ct + 1)
                over_tokens(psA, ones, neg).then_inc(ss_ps, 1)
                for d in range(2):
                    rows = slice(d * HD, (d + 1) * HD)
                    if d:
                        pe.wait_ge(sg_ready, ct * 2 + 1)
                    over_tokens(psB, wl[rows, 0, :], sT[rows, E_WL, :]).then_inc(zw_ps, 1)
                    if d:
                        pe.wait_ge(icl_ready, ct * 2 + 1)
                    else:
                        pe.wait_ge(nrm_ready, ct + 1)
                    over_tokens(psA, wl[rows, 1, :], sT[rows, E_AL, :]).then_inc(za_ps, 1)

                with pe.Fori(0, NC) as j:
                    q = ct * NC + j
                    pe.wait_ge(arr_ready, ct * 2 + 2)
                    for d in range(2):
                        pe.wait_ge(bd_ready[d], q + 1)
                        pe.wait_ge(bd_ready2[d], q + 1)
                        x = BX[d]
                        lo = min(x["a"], x["r"])
                        rhs = BD[d][:, lo:lo + 2, :]
                        nc.tensor.matmul(ps[:, 4 * d, 0:256], BD[d][:, x["b"], :], rhs,
                                         start=True, stop=True)
                        nc.tensor.matmul(ps[:, 4 * d, 256:512], BD[d][:, x["k"], :], rhs,
                                         start=True, stop=True).then_inc(gram[d], 1)
                    for d in range(2):
                        pe.wait_ge(y_ready[d], q + 1)
                        for n, name in enumerate("abkv"):
                            last = nc.tensor.transpose(ps[:, 4 * d + 1, n * P:(n + 1) * P],
                                                       BD[d][:, BX[d][name], :], ident)
                        last.then_inc(bytok[d], 1)
                    for d in range(2):
                        pe.wait_ge(y1_ready[d], q + 1)
                        nc.tensor.transpose(ps[:, 4 * d + 2, 384:512], XY[d][:, 1, :], ident
                                            ).then_inc(x1t[d], 1)
                    for l in range(LEVELS):
                        for d in range(2):
                            if l == 0:
                                pe.wait_ge(lvl_ready[d], q + 1)
                                pe.wait_ge(x1c[d], q + 1)
                            else:
                                pe.wait_ge(xy_ready[d], q * LEVELS + l)
                            nc.tensor.matmul(ps[:, 4 * d + 2, 0:P], ML[d][:, l, :], XY[d][:, 0, :],
                                             start=True, stop=True).then_inc(q_ps[d], 1)
                        if l == 1:
                            for d in range(2):
                                pe.wait_ge(copied[d], q + 1)
                                nc.tensor.matmul(ps[:, 4 * d + 3, 0:P], WK[d][:, GX[d]["ak"], :],
                                                 WK[d][:, 3, :], start=True, stop=True
                                                 ).then_inc(w1_ps[d], 1)
                        for d in range(2):
                            pe.wait_ge(q_ready[d], q * LEVELS + (l + 1))
                            if l < LEVELS - 1:
                                nc.tensor.matmul(ps[:, 4 * d + 2, P:2 * P], XY[d][:, 1, :],
                                                 Q1[d][:, :], start=True, stop=True)
                            nc.tensor.matmul(ps[:, 4 * d + 2, 2 * P:3 * P], Q1[d][:, :],
                                             XY[d][:, 1, :], start=True, stop=True
                                             ).then_inc(xy_ps[d], 1)
                    for d in range(2):
                        pe.wait_ge(w1_ready[d], q + 1)
                        pe.wait_ge(xy_ready[d], q * LEVELS + LEVELS)
                        nc.tensor.matmul(ps[:, 4 * d + 3, P:3 * P], XY[d][:, 1, :],
                                         WK[d][:, 0:5:4, :], start=True, stop=True
                                         ).then_inc(u_ps[d], 1)
                    for d in range(2):
                        rb = GX[d]["rb"]
                        pe.wait_ge(u_ready[d], q + 1)
                        nc.tensor.matmul(ps[:, 4 * d, 0:256], WK[d][:, 9, :],
                                         WK[d][:, 1:rb + 1:rb - 1, :], start=True, stop=True
                                         ).then_inc(m_ps[d], 1)
                    for d in range(2):
                        g = GX[d]
                        pe.wait_ge(m_ready[d], q + 2)
                        pe.wait_ge(s_ready[d], q + 1)
                        yp, sp_ = ps[:, 4 * d + 1, P:2 * P], ps[:, 4 * d + 1, 0:P]
                        nc.tensor.matmul(yp, S[d][:, :], WK[d][:, 12, :], start=True, stop=False)
                        nc.tensor.matmul(yp, WK[d][:, 10, :], WK[d][:, g["rb"], :], start=False, stop=False)
                        nc.tensor.matmul(yp, WK[d][:, 3, :], WK[d][:, g["rk"], :], start=False, stop=True)
                        nc.tensor.matmul(sp_, WK[d][:, 11, :], S[d][:, :], start=True, stop=False)
                        nc.tensor.matmul(sp_, WK[d][:, 1, :], WK[d][:, 10, :], start=False, stop=False)
                        nc.tensor.matmul(sp_, WK[d][:, 2, :], WK[d][:, 3, :], start=False, stop=True
                                         ).then_inc(s_ps[d], 1)

                pe.wait_ge(ysum, ct + 1)
                over_tokens(psA, mean, lw).then_inc(mean_ps, 1)
                pe.wait_ge(ysq, ct + 1)
                over_tokens(psB, mean, neg).then_inc(var_ps, 1)
                pe.wait_ge(bq_ready, ct + 1)
                over_tokens(psA, ones, kds)
                over_tokens(psB, wl[:, 2, :], sT[:, E_GL, :]).then_inc(gb_ps, 1)

        @block.scalar
        def _(act):
            with act.Fori(0, CT) as ct:
                k = sT[:, bass.ds(ct + 4, 1), :]
                act.wait_ge(pc_ready, ct * 2 + 2)
                nc.scalar.activation(kk, k, ACT.Copy, scale=pc[:, K_K:K_K + 1])
                nc.scalar.activation(neg, k, ACT.Square, scale=pc[:, K_K:K_K + 1]).then_inc(sq_ready, 1)
                act.wait_ge(ss_ps, ct + 1)
                nc.scalar.activation(lw, psA[:, 0:T], ACT.Sqrt,
                                     bias=params[:, PM_EPS + 2:PM_EPS + 3]).then_inc(nrm_ready, 1)
                for d in range(2):
                    act.wait_ge(zw_ps, ct * 2 + (d + 1))
                    if d:
                        act.wait_ge(arr_ready, ct * 2 + 1)
                    else:
                        act.wait_ge(kk_ready, ct + 1)
                    nc.scalar.activation(lw, psB[:, 0:T], ACT.Sigmoid,
                                         bias=pc[:, W0A + d:W0A + d + 1]).then_inc(sg_ready, 1)
                    act.wait_ge(za_ps, ct * 2 + (d + 1))
                    nc.scalar.activation(icl, psA[:, 0:T], ACT.Sigmoid,
                                         bias=pc[:, A0A + d:A0A + d + 1]).then_inc(icl_ready, 1)
                    act.wait_ge(cum_ready, ct * 2 + (d + 1))
                    nc.scalar.activation(neg, cum, ACT.Exp, scale=-1.0)
                    nc.scalar.activation(lw, lw, ACT.Exp)
                    nc.scalar.activation(cum, cum, ACT.Exp).then_inc(exps_ready, 1)

                with act.Fori(0, NC) as j:
                    q = ct * NC + j
                    act.wait_ge(arr_ready, ct * 2 + 2)
                    for d in range(2):
                        act.wait_ge(m_ready[d], q + 1)
                        nc.scalar.activation(BD[d][0:C, 1:6, 0:C],
                                             AR[0:C, 4 * d:4 * d + 5, bass.ts(chunk_of(d, j), C)],
                                             ACT.Copy).then_inc(bd_ready[d], 1)
                    for d in range(2):
                        act.wait_ge(bytok[d], q + 1)
                        nc.scalar.activation(WK[d][:, 0:4, :], ps[:, 4 * d + 1, :], ACT.Copy
                                             ).then_inc(copied[d], 1)
                    for d in range(2):
                        act.wait_ge(x1t[d], q + 1)
                        nc.scalar.activation(XY[d][:, 0, :], ps[:, 4 * d + 2, 384:512], ACT.Copy
                                             ).then_inc(x1c[d], 1)
                    for l in range(LEVELS):
                        for d in range(2):
                            act.wait_ge(xy_ps[d], q * LEVELS + (l + 1))
                            h = 0 if l < LEVELS - 1 else 1
                            nc.scalar.activation(XY[d][:, h:2, :],
                                                 ps[:, 4 * d + 2, (1 + h) * P:3 * P], ACT.Copy
                                                 ).then_inc(xy_ready[d], 1)
                    for d in range(2):
                        act.wait_ge(u_ps[d], q + 1)
                        nc.scalar.activation(WK[d][:, 9:11, :], ps[:, 4 * d + 3, P:3 * P], ACT.Copy
                                             ).then_inc(u_ready[d], 1)

                act.wait_ge(yc_ready, ct + 1)
                nc.scalar.activation(neg, lw, ACT.Square).then_inc(ysq, 1)
                act.wait_ge(var_ps, ct + 1)
                nc.scalar.activation(cum, psB[:, 0:T], ACT.Sqrt,
                                     bias=params[:, PM_EPS + 1:PM_EPS + 2]).then_inc(std_ready, 1)

        @block.vector
        def _(dve):
            for d in range(2):
                dve.sem_inc(m_ready[d], 1)
                dve.sem_inc(s_ready[d], 1)
                dve.sem_inc(y_ready[d], 1)
            dve.sem_inc(pdone, 1)
            dve.wait_ge(cs_in, 16)
            dve.wait_ge(zeroed, 6)
            with dve.Fori(0, CT) as ct:
                own = Steps(dve, dch, ct * NDCH)
                r, k, v = (sT[:, bass.ds(ct + 4 * n, 1), :] for n in range(3))
                nc.vector.tensor_copy(pc[:, 0:NPC], params[:, bass.ds(ct * NPC + PM_RK, NPC)]
                                      ).then_inc(pc_ready, 1)
                dve.wait_ge(pc_ready, ct * 2 + 1)
                nc.vector.tensor_scalar(pc[:, K_1A:K_1A + 1], pc[:, K_A:K_A + 1], -1.0, 1.0,
                                        ALU.mult, ALU.add).then_inc(pc_ready, 1)
                nc.vector.tensor_copy(AR[:, V, :], v)
                dve.wait_ge(nrm_ready, ct + 1)
                own.mark(nc.vector.reciprocal(lw, lw))
                own.wait()
                nc.vector.tensor_tensor(kk, kk, lw, ALU.mult).then_inc(kk_ready, 1)
                for d in range(2):
                    x = AX_[d]
                    way = slice(None) if d == 0 else slice(None, None, -1)
                    dve.wait_ge(sg_ready, ct * 2 + (d + 1))
                    own.mark(nc.vector.tensor_scalar(lw, lw, DECAY, None, ALU.mult))
                    own.wait()
                    own.mark(nc.vector.tensor_tensor_scan(cum[:, way], reset, lw[:, way], 0.0,
                                                          ALU.mult, ALU.add))
                    own.wait()
                    nc.vector.tensor_tensor(lw, cum, lw, ALU.subtract).then_inc(cum_ready, 1)
                    dve.wait_ge(icl_ready, ct * 2 + (d + 1))
                    own.mark(nc.vector.tensor_tensor(AR[:, x["b"], :], kk, icl, ALU.mult))
                    own.wait()
                    own.mark(nc.vector.tensor_scalar(icl, icl, pc[:, K_A:K_A + 1],
                                                     pc[:, K_1A:K_1A + 1], ALU.mult, ALU.add))
                    own.wait()
                    own.mark(nc.vector.tensor_tensor(icl, icl, k, ALU.mult))
                    own.wait()
                    if d == 0:
                        nc.vector.tensor_copy(kds, icl)
                    else:
                        nc.vector.tensor_tensor(kds, kds, icl, ALU.add)
                    dve.wait_ge(exps_ready, ct * 2 + (d + 1))
                    nc.vector.scalar_tensor_tensor(AR[:, x["a"], :], kk, -1.0, lw, ALU.mult, ALU.mult)
                    nc.vector.tensor_tensor(AR[:, x["r"], :], r, cum, ALU.mult)
                    at = C - 1 if d == 0 else 0
                    nc.vector.tensor_tensor(edge[:, d, :], cum[:, at:T:C], keep[:, d, :], ALU.mult)
                    nc.vector.tensor_tensor(AR[:, x["b"], :], AR[:, x["b"], :], neg, ALU.mult)
                    nc.vector.tensor_tensor(AR[:, x["k"], :], icl, neg, ALU.mult
                                            ).then_inc(arr_ready, 1)

                with dve.Fori(0, NC) as j:
                    q = ct * NC + j
                    for d in range(2):
                        dve.wait_ge(gram[d], q + 1)
                        nc.vector.tensor_tensor(WK[d][:, 5:9, :], ps[:, 4 * d, :], gmask[d], ALU.mult
                                                ).then_inc(masked[d], 1)
                    for d in range(2):
                        dve.wait_ge(masked[d], q + 1)
                        nc.vector.tensor_tensor(XY[d][:, 1, :], WK[d][:, GX[d]["ab"], :], first[d],
                                                ALU.mult).then_inc(y1h[d], 1)
                    for d in range(2):
                        dve.wait_ge(y1h[d], q + 1)
                        nc.vector.tensor_tensor(XY[d][:, 1, :], XY[d][:, 1, :], ident, ALU.add
                                                ).then_inc(y1_ready[d], 1)
                    for l in range(LEVELS):
                        for d in range(2):
                            dve.wait_ge(q_ps[d], q * LEVELS + (l + 1))
                            nc.vector.tensor_tensor(Q1[d][:, :], ps[:, 4 * d + 2, 0:P], ident, ALU.add
                                                    ).then_inc(q_ready[d], 1)
                        if l == 1:
                            for d in range(2):
                                dve.wait_ge(w1_ps[d], q + 1)
                                nc.vector.tensor_copy(WK[d][:, 4, :], ps[:, 4 * d + 3, 0:P]
                                                      ).then_inc(w1_ready[d], 1)
                    for d in range(2):
                        r_ = BX[d]["r"]
                        dve.wait_ge(m_ps[d], q + 1)
                        nc.vector.tensor_tensor(WK[d][:, 11:13, :], ps[:, 4 * d, 0:256],
                                                BD[d][:, 0:r_ + 1:r_, :], ALU.add
                                                ).then_inc(m_ready[d], 1)
                    for d in range(2):
                        c = chunk_of(d, j)
                        dve.wait_ge(s_ps[d], q + 1)
                        nc.vector.tensor_scalar(S[d][:, :], ps[:, 4 * d + 1, 0:P],
                                                edge[:, d, bass.ds(c, 1)], None, ALU.mult
                                                ).then_inc(s_ready[d], 1)
                        nc.vector.tensor_reduce(
                            y[d][:, bass.ts(c, C)],
                            ps[:, 4 * d + 1, P:2 * P].rearrange("p (h t) -> p t h", h=2),
                            AX.X, ALU.add).then_inc(y_ready[d], 1)

                for d in range(2):
                    dve.wait_ge(y_ready[d], ct * NC + NC + 1)
                nc.vector.tensor_tensor(lw, lw, cum, ALU.add).then_inc(ysum, 1)
                dve.wait_ge(mean_ps, ct + 1)
                nc.vector.tensor_tensor(lw, lw, psA[:, 0:T], ALU.subtract).then_inc(yc_ready, 1)
                nc.vector.scalar_tensor_tensor(kds, r, pc[:, R_K:R_K + 1], kds, ALU.mult, ALU.mult)
                dve.wait_ge(std_ready, ct + 1)
                own.mark(nc.vector.reciprocal(cum, cum))
                own.wait()
                own.mark(nc.vector.tensor_tensor(lw, lw, cum, ALU.mult))
                own.wait()
                nc.vector.tensor_scalar(lw, lw, pc[:, LN_W:LN_W + 1], pc[:, LN_B:LN_B + 1],
                                        ALU.mult, ALU.add).then_inc(bq_ready, 1)
                dve.wait_ge(gb_ps, ct + 1)
                own.mark(nc.vector.tensor_tensor(icl, v, psA[:, 0:T], ALU.mult))
                own.wait()
                own.mark(nc.vector.tensor_tensor(lw, lw, icl, ALU.add))
                own.wait()
                nc.vector.tensor_tensor(r, lw, psB[:, 0:T], ALU.mult).then_inc(pdone, 1)
                assert own.n == NDCH, own.n
                dve.wait_ge(pdone, ct + 2)

    nc.clear_and_free_semaphores(sems)
    nc.all_engine_barrier()


def attention_projection(nc, w_in, w_v, hT_dram, v_dram, hT, qk):
    E_QK = 2 * CT
    with ExitStack() as ctx:
        sb = lambda n, s: ctx.enter_context(nc.sbuf_tensor(n, s, F32))
        sem = lambda n: ctx.enter_context(nc.semaphore("ap_" + n))
        w = [sb(f"ap_w{j}", [P, D]) for j in range(2)]
        wv = sb("ap_wv", [P, KD, 512])
        vt = [sb(f"ap_vt{j}", [P, 512]) for j in range(2)]
        ps = [ctx.enter_context(nc.psum_tensor(f"ap_ps{j}", [P, 1536], F32)) for j in range(2)]
        pv = [ctx.enter_context(nc.psum_tensor(f"ap_pv{j}", [P, 512], F32)) for j in range(2)]
        w_ld = [sem(f"w_ld{j}") for j in range(2)]
        v_out = [sem(f"v_out{j}") for j in range(2)]
        h_in, wv_in, gemm, qk_ready, v_ps, v_ready = (
            sem("h_in"), sem("wv_in"), sem("gemm"), sem("qk"), sem("v_ps"), sem("v"))
        block = ctx.enter_context(nc.Block())

        @block.sync
        def _(sp):
            sp.dma_start(hT.rearrange("p k t -> p (k t)"), hT_dram).then_inc(h_in, 16)
            with sp.Fori(0, E_QK // 2) as i:
                for j in range(2):
                    e = i * 2 + j
                    sp.wait_ge(gemm, e * NG + NG)
                    sp.dma_start(w[j][:, :], w_in[e, :, :]).then_inc(w_ld[j], 16)
            sp.dma_start(wv[:, :, :], w_v).then_inc(wv_in, 16)
            for n in range(NT):
                sp.wait_ge(v_ready, n + 1)
                sp.dma_start(v_dram[n * P:(n + 1) * P, :], vt[n % 2][:, :]).then_inc(v_out[n % 2], 16)
            for j in range(2):
                sp.wait_ge(v_out[j], 16 * (NT // 2))

        @block.tensor
        def _(pe):
            pe.sem_inc(gemm, 2 * NG)
            pe.wait_ge(h_in, 16)
            with pe.Fori(0, E_QK // 2) as i:
                for j in range(2):
                    e = i * 2 + j
                    pe.wait_ge(w_ld[j], i * 16 + 16)
                    for g, (t0, tn) in enumerate(GROUPS):
                        pe.wait_ge(qk_ready, e * NG + (g + 1))
                        for k in range(KD):
                            last = nc.tensor.matmul(ps[j][:, t0:t0 + tn], w[j][:, k * P:(k + 1) * P],
                                                    hT[:, k, t0:t0 + tn], start=k == 0, stop=k == KD - 1)
                        last.then_inc(gemm, 1)
            pe.wait_ge(wv_in, 16)
            for n in range(NT):
                if n >= 2:
                    pe.wait_ge(v_ready, n - 1)
                for k in range(KD):
                    last = nc.tensor.matmul(pv[n % 2][:, :], hT[:, k, n * P:(n + 1) * P], wv[:, k, :],
                                            start=k == 0, stop=k == KD - 1)
                last.then_inc(v_ps, 1)

        @block.scalar
        def _(act):
            act.sem_inc(qk_ready, 2 * NG)
            with act.Fori(0, E_QK // 2) as i:
                for j in range(2):
                    e = i * 2 + j
                    for g, (t0, tn) in enumerate(GROUPS):
                        act.wait_ge(gemm, e * NG + (2 * NG + g + 1))
                        nc.scalar.activation(qk[:, bass.ds(e, 1), t0:t0 + tn], ps[j][:, t0:t0 + tn],
                                             ACT.Copy).then_inc(qk_ready, 1)
            act.wait_ge(qk_ready, E_QK * NG + 2 * NG)

        @block.vector
        def _(dve):
            for n in range(NT):
                if n >= 2:
                    dve.wait_ge(v_out[n % 2], 16 * (n // 2))
                dve.wait_ge(v_ps, n + 1)
                nc.vector.tensor_copy(vt[n % 2][:, :], pv[n % 2][:, :]).then_inc(v_ready, 1)


def attention(nc, rpb, cm, v_dram, ident, qk, oT):
    ROWS = []
    for base, tokens in ((0, TP), (TP, TS)):
        rows = tokens // GRID_W
        kh = min(WIN_H, rows)
        for r in range(rows):
            r0 = min(max(r - kh // 2, 0), rows - kh)
            ROWS.append((base + r * GRID_W, base + r0 * GRID_W, kh * GRID_W, r0 - r + WIN_H - 1))
    NR, NDR = len(ROWS), 2 * WIN_H - 1
    NODD = (TP - GRID_W) // P

    def backwards(h):
        return slice(h * GRID_W + GRID_W - 1, h * GRID_W - 1 if h else None, -1)

    with ExitStack() as ctx:
        sb = lambda n, s: ctx.enter_context(nc.sbuf_tensor(n, s, F32))
        sem = lambda n: ctx.enter_context(nc.semaphore("at_" + n))
        bias = sb("at_bias", [P, CT, NDR * GRID_W])
        cms = sb("at_cm", [P, GRID_W])
        v_even, v_odd = sb("at_ve", [P, NT, P]), sb("at_vo", [P, NODD, P])
        qb = [sb(f"at_qb{j}", [P, P]) for j in range(2)]
        sc = [sb(f"at_sc{j}", [P, 512]) for j in range(2)]
        pr = [sb(f"at_pr{j}", [P, 512]) for j in range(2)]
        prT = [sb(f"at_prT{j}", [P, 512]) for j in range(2)]
        st = [sb(f"at_st{j}", [P, 4]) for j in range(2)]
        pb = lambda n: [ctx.enter_context(nc.psum_tensor(f"at_{n}{j}", [P, 512], F32)) for j in range(2)]
        s_ps, t_ps, o_ps = pb("s"), pb("t"), pb("o")
        bias_in, bias_ready, zeroed, v_in = sem("bias_in"), sem("bias"), sem("zeroed"), sem("v_in")
        q_ready, scores, biased, maxed, shift_ready, exped, summed, normed = (
            sem("q"), sem("scores"), sem("biased"), sem("maxed"), sem("shift"), sem("exp"),
            sem("sum"), sem("norm"))
        turned, turned_c, pv_done, o_ready = sem("turned"), sem("turned_c"), sem("pv"), sem("o")
        block = ctx.enter_context(nc.Block())

        @block.sync
        def _(sp):
            with nc.allow_non_contiguous_dma(reason="v tiles of a head pair"):
                with sp.Fori(0, CT) as p:
                    sp.wait_ge(pv_done, p * NR + 2)
                    sp.dma_start(v_even[:, :, :], v_dram.rearrange("(n p) c -> p n c", p=P)
                                 [:, :, bass.ts(p, P)]).then_inc(v_in, 16)
                    sp.dma_start(v_odd[:, :, :], v_dram[GRID_W:GRID_W + NODD * P, :]
                                 .rearrange("(n p) c -> p n c", p=P)[:, :, bass.ts(p, P)]
                                 ).then_inc(v_in, 16)

        @block.gpsimd
        def _(pool):
            for j in range(2):
                nc.gpsimd.memset(qb[j][:, :], 0.0).then_inc(zeroed, 1)
            pool.wait_ge(zeroed, 2)
            with pool.Fori(0, CT) as p:
                for r, (q0, k0, nk, dr) in enumerate(ROWS):
                    n, j = p * NR + r, r % 2
                    pool.wait_ge(scores, n + 1)
                    for h in range(2):
                        rows = slice(h * HD, (h + 1) * HD)
                        nc.gpsimd.tensor_copy(qb[j][rows, backwards(h)],
                                              qk[rows, bass.ds(p, 1), q0:q0 + GRID_W]
                                              ).then_inc(q_ready, 1)

        @block.tensor
        def _(pe):
            pe.sem_inc(scores, 2)
            pe.sem_inc(turned, 2)
            pe.sem_inc(pv_done, 2)
            with pe.Fori(0, CT) as p:
                for step in range(NR + 2):
                    if step < NR:
                        q0, k0, nk, dr = ROWS[step]
                        n, j = p * NR + step, step % 2
                        pe.wait_ge(q_ready, n * 2 + 2)
                        pe.wait_ge(biased, n + 1)
                        nc.tensor.matmul(s_ps[j][:, 0:nk], qb[j][:, :], qk[:, bass.ds(p + CT, 1), k0:k0 + nk],
                                         start=True, stop=True).then_inc(scores, 1)
                    if 1 <= step <= NR:
                        q0, k0, nk, dr = ROWS[step - 1]
                        n, j = p * NR + (step - 1), (step - 1) % 2
                        pe.wait_ge(normed, n + 1)
                        pe.wait_ge(turned_c, n + 1)
                        for m in range(nk // P):
                            last = nc.tensor.transpose(t_ps[j][:, m * P:(m + 1) * P],
                                                       pr[j][:, m * P:(m + 1) * P], ident)
                        last.then_inc(turned, 1)
                    if step >= 2:
                        q0, k0, nk, dr = ROWS[step - 2]
                        n, j = p * NR + (step - 2), step % 2
                        if step == 2:
                            pe.wait_ge(v_in, p * 32 + 32)
                        pe.wait_ge(turned_c, n + 3)
                        pe.wait_ge(o_ready, n + 1)
                        for m in range(nk // P):
                            at = k0 + m * P
                            v = v_even[:, at // P, :] if at % P == 0 else v_odd[:, (at - GRID_W) // P, :]
                            last = nc.tensor.matmul(o_ps[j][:, 0:P], v, prT[j][:, m * P:(m + 1) * P],
                                                    start=m == 0, stop=m == nk // P - 1)
                        last.then_inc(pv_done, 1)

        @block.scalar
        def _(act):
            act.sem_inc(exped, 2)
            act.sem_inc(turned_c, 2)
            with nc.allow_non_contiguous_dma(reason="bias rows, one shifted row for a query column"):
                for h in range(2 * CT):
                    rows = slice(h % 2 * GRID_W, (h % 2 + 1) * GRID_W)
                    width = 2 * GRID_W - 1
                    src = rpb[h, :, 0:GRID_W]
                    src = bass.AP(tensor=src.tensor, offset=src.offset,
                                  ap=[[1, GRID_W], [width, NDR], [1, GRID_W]])
                    act.dma_start(bias[rows, h // 2, :].rearrange("p (r c) -> p r c", c=GRID_W), src
                                  ).then_inc(bias_in, 16)
                act.dma_start(cms[:, :], cm).then_inc(bias_in, 16)
            with act.Fori(0, CT) as p:
                for step in range(NR + 1):
                    if step < NR:
                        nk = ROWS[step][2]
                        n, j = p * NR + step, step % 2
                        act.wait_ge(shift_ready, n + 1)
                        act.wait_ge(turned, n + 1)
                        nc.scalar.activation(pr[j][:, 0:nk], sc[j][:, 0:nk], ACT.Exp, bias=st[j][:, 1:2],
                                             accum_out=st[j][:, 2:3]).then_inc(exped, 1)
                    if step >= 1:
                        nk = ROWS[step - 1][2]
                        n, j = p * NR + (step - 1), (step - 1) % 2
                        act.wait_ge(turned, n + 3)
                        act.wait_ge(pv_done, n + 1)
                        nc.scalar.activation(prT[j][:, 0:nk], t_ps[j][:, 0:nk], ACT.Copy
                                             ).then_inc(turned_c, 1)

        @block.vector
        def _(dve):
            dve.sem_inc(biased, 2)
            dve.sem_inc(o_ready, 2)
            dve.wait_ge(bias_in, 16 * 9)
            flat = bias[:, :, :].rearrange("p n (r c) -> p (n r) c", c=GRID_W)
            nc.vector.tensor_tensor(flat, flat, cms[:, :].unsqueeze(1).to_broadcast([P, CT * NDR, GRID_W]),
                                    ALU.add).then_inc(bias_ready, 1)
            dve.wait_ge(bias_ready, 1)
            with dve.Fori(0, CT) as p:
                for step in range(NR + 2):
                    if step < NR:
                        q0, k0, nk, dr = ROWS[step]
                        n, j = p * NR + step, step % 2
                        dve.wait_ge(scores, n + 3)
                        dve.wait_ge(exped, n + 1)
                        nc.vector.scalar_tensor_tensor(
                            sc[j][:, 0:nk], s_ps[j][:, 0:nk], HD ** -0.5,
                            bias[:, bass.ds(p, 1), dr * GRID_W:dr * GRID_W + nk],
                            ALU.mult, ALU.add).then_inc(biased, 1)
                        dve.wait_ge(biased, n + 3)
                        nc.vector.reduce_max(st[j][:, 0:1], sc[j][:, 0:nk], AX.X).then_inc(maxed, 1)
                        dve.wait_ge(maxed, n + 1)
                        nc.vector.tensor_scalar(st[j][:, 1:2], st[j][:, 0:1], -1.0, None, ALU.mult
                                                ).then_inc(shift_ready, 1)
                    if 1 <= step <= NR:
                        nk = ROWS[step - 1][2]
                        n, j = p * NR + (step - 1), (step - 1) % 2
                        dve.wait_ge(exped, n + 3)
                        nc.vector.reciprocal(st[j][:, 3:4], st[j][:, 2:3]).then_inc(summed, 1)
                        dve.wait_ge(summed, n + 1)
                        nc.vector.tensor_scalar(pr[j][:, 0:nk], pr[j][:, 0:nk], st[j][:, 3:4], None,
                                                ALU.mult).then_inc(normed, 1)
                    if step >= 2:
                        q0 = ROWS[step - 2][0]
                        n, j = p * NR + (step - 2), step % 2
                        dve.wait_ge(pv_done, n + 3)
                        for h in range(2):
                            rows = slice(h * HD, (h + 1) * HD)
                            last = nc.vector.tensor_scalar(oT[rows, bass.ds(p, 1), q0:q0 + GRID_W],
                                                           o_ps[j][rows, backwards(h)], 1.0, None,
                                                           ALU.mult)
                        last.then_inc(o_ready, 1)
            dve.wait_ge(o_ready, CT * NR + 2)


def merge_branches(nc, w_merge, params, hT, oaT, obT, mT):
    with ExitStack() as ctx:
        sb = lambda n, s: ctx.enter_context(nc.sbuf_tensor(n, s, F32))
        sem = lambda n: ctx.enter_context(nc.semaphore("mb_" + n))
        w = [sb(f"mb_w{j}", [P, 3 * D + 2]) for j in range(2)]
        gate = [sb(f"mb_gate{j}", [P, 2, 512]) for j in range(2)]
        part = [sb(f"mb_part{j}", [P, 2, 512]) for j in range(2)]
        ps = [ctx.enter_context(nc.psum_tensor(f"mb_ps{j}", [P, 4, 512], F32)) for j in range(2)]
        w_ld = [sem(f"w_ld{j}") for j in range(2)]
        gemm, gated, parts, merged = sem("gemm"), sem("gated"), sem("parts"), sem("merged")
        block = ctx.enter_context(nc.Block())

        @block.sync
        def _(sp):
            with sp.Fori(0, KD // 2) as i:
                for j in range(2):
                    c = i * 2 + j
                    sp.wait_ge(merged, c * NG + 1)
                    sp.dma_start(w[j][:, :], w_merge[c, :, :]).then_inc(w_ld[j], 16)

        @block.tensor
        def _(pe):
            with pe.Fori(0, KD // 2) as i:
                for j in range(2):
                    for g, (t0, tn) in enumerate(GROUPS):
                        u, b = (i * 2 + j) * NG + g, (j * NG + g) % 2
                        if g == 0:
                            pe.wait_ge(w_ld[j], i * 16 + 16)
                        pe.wait_ge(merged, u + 3)
                        at = 0
                        for out, (src, tiles) in enumerate(((hT, KD), (hT, KD), (oaT, CT), (obT, CT))):
                            for k in range(tiles):
                                last = nc.tensor.matmul(ps[b][:, out, 0:tn], w[j][:, at:at + P],
                                                        src[:, k, t0:t0 + tn],
                                                        start=k == 0, stop=k == tiles - 1)
                                at += P
                        last.then_inc(gemm, 1)

        @block.scalar
        def _(act):
            with act.Fori(0, KD // 2) as i:
                for j in range(2):
                    c = i * 2 + j
                    for g, (t0, tn) in enumerate(GROUPS):
                        u, b = c * NG + g, (j * NG + g) % 2
                        act.wait_ge(gemm, u + 1)
                        act.wait_ge(merged, u + 3)
                        for h in range(2):
                            nc.scalar.activation(gate[b][:, h, 0:tn], ps[b][:, h, 0:tn], ACT.Sigmoid,
                                                 bias=w[j][:, 3 * D + h:3 * D + h + 1]
                                                 ).then_inc(gated, 1)

        @block.vector
        def _(dve):
            dve.sem_inc(merged, 1 + NG)
            with dve.Fori(0, KD // 2) as i:
                for j in range(2):
                    c = i * 2 + j
                    for g, (t0, tn) in enumerate(GROUPS):
                        u, b = c * NG + g, (j * NG + g) % 2
                        dve.wait_ge(gated, u * 2 + 2)
                        nc.vector.tensor_tensor(part[b][:, :, 0:tn], gate[b][:, :, 0:tn],
                                                ps[b][:, 2:4, 0:tn], ALU.mult).then_inc(parts, 1)
                        dve.wait_ge(parts, u + 1)
                        nc.vector.tensor_tensor(mT[:, bass.ds(c, 1), t0:t0 + tn], part[b][:, 0, 0:tn],
                                                part[b][:, 1, 0:tn], ALU.add).then_inc(merged, 1)
            dve.wait_ge(merged, KD * NG + 1 + NG)


def output_projection(nc, x, w_out, gains, params, ident, mT, wo, x1_dram, hT):
    with ExitStack() as ctx:
        sb = lambda n, s: ctx.enter_context(nc.sbuf_tensor(n, s, F32))
        sem = lambda n: ctx.enter_context(nc.semaphore("op_" + n))
        xs = [sb(f"op_x{j}", [P, D]) for j in range(2)]
        ms = [sb(f"op_m{j}", [P, KD, P]) for j in range(2)]
        yb = [sb(f"op_y{j}", [P, D]) for j in range(2)]
        gain, sq = sb("op_gain", [P, D]), sb("op_sq", [P, D])
        xo = [sb(f"op_xo{j}", [P, D]) for j in range(2)]
        st = [sb(f"op_st{j}", [P, 6]) for j in range(2)]
        pg = [ctx.enter_context(nc.psum_tensor(f"op_pg{j}", [P, D], F32)) for j in range(2)]
        pt = [ctx.enter_context(nc.psum_tensor(f"op_pt{j}", [P, D], F32)) for j in range(2)]
        x_in = [sem(f"x_in{j}") for j in range(2)]
        x_out = [sem(f"x_out{j}") for j in range(2)]
        stored = sem("stored")
        w_ld, g_in, staged, gemm, sq1, rms1, inv1, scaled, x1_ready = (
            sem("w_ld"), sem("g_in"), sem("staged"), sem("gemm"), sem("sq1"), sem("rms1"),
            sem("inv1"), sem("scaled"), sem("x1"))
        sq2, rms2, inv2, xn_ready, turned, h_ready = (
            sem("sq2"), sem("rms2"), sem("inv2"), sem("xn"), sem("turned"), sem("h"))
        xr = x.rearrange("(n p) d -> n p d", p=P)
        x1r = x1_dram.rearrange("(n p) d -> n p d", p=P)
        block = ctx.enter_context(nc.Block())

        @block.sync
        def _(sp):
            sp.dma_start(wo, w_out).then_inc(w_ld, 16)
            sp.dma_start(gain[:, :], gains[0, :].partition_broadcast(P)).then_inc(g_in, 16)
            with sp.Fori(0, NT // 2) as i:
                for j in range(2):
                    n = i * 2 + j
                    sp.wait_ge(x1_ready, n + 1)
                    sp.dma_start(xs[j][:, :], xr[n, :, :]).then_inc(x_in[j], 16)

        @block.gpsimd
        def _(pool):
            pool.sem_inc(stored, 2)
            with pool.Fori(0, NT // 2) as i:
                for j in range(2):
                    n = i * 2 + j
                    pool.wait_ge(gemm, n + 1)
                    nc.gpsimd.tensor_copy(ms[j][:, :, :], mT[:, :, bass.ts(n, P)]).then_inc(staged, 1)
                    pool.wait_ge(x1_ready, n + 3)
                    pool.dma_start(x1r[n, :, :], xo[j][:, :]).then_inc(x_out[j], 16)
                    pool.wait_ge(x_out[j], i * 16 + 16)
                    pool.sem_inc(stored, 1)

        @block.tensor
        def _(pe):
            pe.sem_inc(gemm, 2)
            pe.sem_inc(turned, 2)
            pe.wait_ge(w_ld, 16)

            def project(n, j):
                pe.wait_ge(staged, n + 1)
                pe.wait_ge(scaled, n + 1)
                for h in range(2):
                    for k in range(KD):
                        last = nc.tensor.matmul(pg[j][:, h * 512:(h + 1) * 512], ms[j][:, k, :],
                                                wo[:, k, h * 512:(h + 1) * 512],
                                                start=k == 0, stop=k == KD - 1)
                last.then_inc(gemm, 1)

            def turn(n, j):
                pe.wait_ge(xn_ready, n + 3)
                pe.wait_ge(h_ready, n + 1)
                for k in range(KD):
                    last = nc.tensor.transpose(pt[j][:, k * P:(k + 1) * P],
                                               yb[j][:, k * P:(k + 1) * P], ident)
                last.then_inc(turned, 1)

            project(0, 0)
            with pe.Fori(0, NT // 2 - 1) as i:
                for j in range(2):
                    project(i * 2 + (j + 1), 1 - j)
                    turn(i * 2 + j, j)
            project(NT - 1, 1)
            turn(NT - 2, 0)
            turn(NT - 1, 1)

        @block.scalar
        def _(act):
            with act.Fori(0, NT // 2) as i:
                for j in range(2):
                    n = i * 2 + j
                    s = st[j]
                    act.wait_ge(gemm, n + 3)
                    nc.scalar.activation(sq[:, :], pg[j][:, :], ACT.Square, accum_out=s[:, 0:1]
                                         ).then_inc(sq1, 1)
                    act.wait_ge(sq1, n + 1)
                    nc.scalar.activation(s[:, 1:2], s[:, 0:1], ACT.Sqrt, scale=1.0 / D,
                                         bias=params[:, PM_EPS:PM_EPS + 1]).then_inc(rms1, 1)
                    act.wait_ge(x1_ready, n + 3)
                    nc.scalar.activation(sq[:, :], xo[j][:, :], ACT.Square, accum_out=s[:, 3:4]
                                         ).then_inc(sq2, 1)
                    act.wait_ge(sq2, n + 1)
                    nc.scalar.activation(s[:, 4:5], s[:, 3:4], ACT.Sqrt, scale=1.0 / D,
                                         bias=params[:, PM_EPS:PM_EPS + 1]).then_inc(rms2, 1)

        @block.vector
        def _(dve):
            for s in (scaled, x1_ready, xn_ready, h_ready):
                dve.sem_inc(s, 2)
            dve.wait_ge(g_in, 16)

            def finish(n, j):
                dve.wait_ge(turned, n + 3)
                nc.vector.tensor_tensor(
                    hT[:, :, bass.ts(n, P)], pt[j][:, :].rearrange("p (k t) -> p k t", k=KD),
                    params[:, PM_G2:PM_G2 + KD].unsqueeze(2).to_broadcast([P, KD, P]),
                    ALU.mult).then_inc(h_ready, 1)

            with dve.Fori(0, NT // 2) as i:
                for j in range(2):
                    n = i * 2 + j
                    s = st[j]
                    dve.wait_ge(rms1, n + 1)
                    nc.vector.reciprocal(s[:, 2:3], s[:, 1:2]).then_inc(inv1, 1)
                    dve.wait_ge(inv1, n + 1)
                    dve.wait_ge(turned, n + 1)
                    nc.vector.scalar_tensor_tensor(yb[j][:, :], pg[j][:, :], s[:, 2:3], gain[:, :],
                                                   ALU.mult, ALU.mult).then_inc(scaled, 1)
                    dve.wait_ge(scaled, n + 3)
                    dve.wait_ge(x_in[j], i * 16 + 16)
                    dve.wait_ge(stored, n + 1)
                    nc.vector.tensor_tensor(xo[j][:, :], yb[j][:, :], xs[j][:, :], ALU.add
                                            ).then_inc(x1_ready, 1)
                    dve.wait_ge(rms2, n + 1)
                    nc.vector.reciprocal(s[:, 5:6], s[:, 4:5]).then_inc(inv2, 1)
                    dve.wait_ge(inv2, n + 1)
                    nc.vector.tensor_scalar(yb[j][:, :], xo[j][:, :], s[:, 5:6], None, ALU.mult
                                            ).then_inc(xn_ready, 1)
                    finish(n, j)
            dve.wait_ge(h_ready, NT + 2)


def feed_forward(nc, w_up, w_down, gains, params, hT, gT, f, x1_dram, out):
    with ExitStack() as ctx:
        sb = lambda n, s: ctx.enter_context(nc.sbuf_tensor(n, s, F32))
        sem = lambda n: ctx.enter_context(nc.semaphore("ff_" + n))
        wu = [sb(f"ff_wu{j}", [P, D]) for j in range(2)]
        wd = sb("ff_wd", [P, FT, D])
        rl = [sb(f"ff_rl{j}", [P, 512]) for j in range(2)]
        pu = [ctx.enter_context(nc.psum_tensor(f"ff_pu{j}", [P, 512], F32)) for j in range(3)]
        pd = [ctx.enter_context(nc.psum_tensor(f"ff_pd{j}", [P, 512], F32)) for j in range(2)]
        u_ld = [sem(f"u_ld{j}") for j in range(2)]
        d_ld, up, relu, act_done, zeroed, down, added = (
            sem("d_ld"), sem("up"), sem("relu"), sem("act"), sem("zeroed"), sem("down"), sem("added"))
        NU, ND = FT * NG, NT * 2
        block = ctx.enter_context(nc.Block())

        @block.sync
        def _(sp):
            with sp.Fori(0, FG) as g:
                for m in range(FT):
                    sp.wait_ge(up, g * NU + (m + 1) * NG)
                    sp.dma_start(wu[m % 2][:, :], w_up[g * FT + m, :, :]).then_inc(u_ld[m % 2], 16)
                    if m == 1:
                        sp.wait_ge(down, g * ND + 1)
                        sp.dma_start(wd[:, :, :], w_down[g, :, :, :]).then_inc(d_ld, 16)

        @block.tensor
        def _(pe):
            pe.sem_inc(up, 2 * NG)
            pe.sem_inc(down, 1)
            with pe.Fori(0, FG) as g:
                for m in range(FT):
                    pe.wait_ge(u_ld[m % 2], g * (FT // 2 * 16) + (m // 2 + 1) * 16)
                    for b, (t0, tn) in enumerate(GROUPS):
                        pe.wait_ge(relu, g * NU + (m * NG + b + 1))
                        for k in range(KD):
                            last = nc.tensor.matmul(pu[b][:, 0:tn], wu[m % 2][:, k * P:(k + 1) * P],
                                                    hT[:, k, t0:t0 + tn], start=k == 0, stop=k == KD - 1)
                        last.then_inc(up, 1)
                pe.wait_ge(d_ld, g * 16 + 16)
                pe.wait_ge(act_done, g * NU + NU + 2)
                for n in range(NT):
                    for h in range(2):
                        pe.wait_ge(added, g * ND + (2 * n + h + 1))
                        for m in range(FT):
                            last = nc.tensor.matmul(pd[h][:, :], gT[:, m, n * P:(n + 1) * P],
                                                    wd[:, m, h * 512:(h + 1) * 512],
                                                    start=m == 0, stop=m == FT - 1)
                        last.then_inc(down, 1)

        @block.scalar
        def _(act):
            act.sem_inc(relu, 3)
            with act.Fori(0, FG) as g:
                for m in range(FT):
                    for b, (t0, tn) in enumerate(GROUPS):
                        u = m * NG + b
                        act.wait_ge(up, g * NU + (2 * NG + u + 1))
                        act.wait_ge(act_done, g * NU + (u + 1))
                        nc.scalar.activation(rl[u % 2][:, 0:tn], pu[b][:, 0:tn], ACT.Relu
                                             ).then_inc(relu, 1)

        @block.vector
        def _(dve):
            dve.sem_inc(added, 2)
            dve.sem_inc(act_done, 2)
            nc.vector.memset(f, 0.0).then_inc(zeroed, 1)
            dve.wait_ge(zeroed, 1)
            with dve.Fori(0, FG) as g:
                for m in range(FT):
                    for b, (t0, tn) in enumerate(GROUPS):
                        u = m * NG + b
                        dve.wait_ge(relu, g * NU + (u + 4))
                        if u == 0:
                            dve.wait_ge(down, g * ND + 1)
                        nc.vector.tensor_tensor(gT[:, m, t0:t0 + tn], rl[u % 2][:, 0:tn],
                                                rl[u % 2][:, 0:tn], ALU.mult).then_inc(act_done, 1)
                for n in range(NT):
                    for h in range(2):
                        dve.wait_ge(down, g * ND + (2 * n + h + 2))
                        at = f[:, n, h * 512:(h + 1) * 512]
                        nc.vector.tensor_tensor(at, at, pd[h][:, :], ALU.add).then_inc(added, 1)
            dve.wait_ge(added, FG * ND + 2)


def final_norm(nc, gains, params, f, x1_dram, out):
    with ExitStack() as ctx:
        sb = lambda n, s: ctx.enter_context(nc.sbuf_tensor(n, s, F32))
        sem = lambda n: ctx.enter_context(nc.semaphore("fn_" + n))
        gain, sq = sb("fn_gain", [P, D]), sb("fn_sq", [P, D])
        xs = [sb(f"fn_x{j}", [P, D]) for j in range(2)]
        ob = [sb(f"fn_o{j}", [P, D]) for j in range(2)]
        st = [sb(f"fn_st{j}", [P, 3]) for j in range(2)]
        x_in = [sem(f"x_in{j}") for j in range(2)]
        o_out = [sem(f"o_out{j}") for j in range(2)]
        stored = sem("stored")
        g_in, squared, rms, inv, scaled, o_ready = (
            sem("g_in"), sem("sq"), sem("rms"), sem("inv"), sem("scaled"), sem("o"))
        x1r = x1_dram.rearrange("(n p) d -> n p d", p=P)
        outr = out.rearrange("(n p) d -> n p d", p=P)
        block = ctx.enter_context(nc.Block())

        @block.sync
        def _(sp):
            sp.dma_start(gain[:, :], gains[1, :].partition_broadcast(P)).then_inc(g_in, 16)
            with sp.Fori(0, NT // 2) as i:
                for j in range(2):
                    n = i * 2 + j
                    sp.wait_ge(o_ready, n + 1)
                    sp.dma_start(xs[j][:, :], x1r[n, :, :]).then_inc(x_in[j], 16)

        @block.gpsimd
        def _(pool):
            pool.sem_inc(stored, 2)
            with pool.Fori(0, NT // 2) as i:
                for j in range(2):
                    n = i * 2 + j
                    pool.wait_ge(o_ready, n + 3)
                    pool.dma_start(outr[n, :, :], ob[j][:, :]).then_inc(o_out[j], 16)
                    pool.wait_ge(o_out[j], i * 16 + 16)
                    pool.sem_inc(stored, 1)

        @block.scalar
        def _(act):
            with act.Fori(0, NT // 2) as i:
                for j in range(2):
                    n = i * 2 + j
                    act.wait_ge(scaled, n + 1)
                    nc.scalar.activation(sq[:, :], f[:, bass.ds(n, 1), :], ACT.Square,
                                         accum_out=st[j][:, 0:1]).then_inc(squared, 1)
                    act.wait_ge(squared, n + 1)
                    nc.scalar.activation(st[j][:, 1:2], st[j][:, 0:1], ACT.Sqrt, scale=1.0 / D,
                                         bias=params[:, PM_EPS:PM_EPS + 1]).then_inc(rms, 1)

        @block.vector
        def _(dve):
            dve.sem_inc(o_ready, 2)
            dve.sem_inc(scaled, 2)
            dve.wait_ge(g_in, 16)
            with dve.Fori(0, NT // 2) as i:
                for j in range(2):
                    n = i * 2 + j
                    dve.wait_ge(rms, n + 1)
                    nc.vector.reciprocal(st[j][:, 2:3], st[j][:, 1:2]).then_inc(inv, 1)
                    dve.wait_ge(inv, n + 1)
                    dve.wait_ge(stored, n + 1)
                    nc.vector.scalar_tensor_tensor(ob[j][:, :], f[:, bass.ds(n, 1), :], st[j][:, 2:3],
                                                   gain[:, :], ALU.mult, ALU.mult).then_inc(scaled, 1)
                    dve.wait_ge(scaled, n + 3)
                    dve.wait_ge(x_in[j], i * 16 + 16)
                    nc.vector.tensor_tensor(ob[j][:, :], ob[j][:, :], xs[j][:, :], ALU.add
                                            ).then_inc(o_ready, 1)


def encoder(nc, a, out, stop=99, dump=None):
    dram = lambda n, s: nc.dram_tensor(n, s, F32).ap()
    hT_dram, v_dram, x1_dram = dram("hT_dram", [P, KD * T]), dram("v_dram", [T, 512]), dram("x1_dram", [T, D])
    with ExitStack() as ctx:
        sb = lambda n, s: ctx.enter_context(nc.sbuf_tensor(n, s, F32))
        sem = lambda n: ctx.enter_context(nc.semaphore(n))
        params, cn = sb("params", [P, PM_N]), sb("cn", [P, CN_N])
        ab = sb("ab", [P, 2 * KD * T])
        sT = sb("sT", [P, E_SH, T])
        ident, ones, mean = (cn[:, c:c + P] for c in (CN_ID, CN_ONES, CN_MEAN))
        hT = ab[:, 0:KD * T].rearrange("p (k t) -> p k t", k=KD)
        other = ab[:, KD * T:2 * KD * T].rearrange("p (k t) -> p k t", k=KD)
        flat = sT[:, :, :].rearrange("p e t -> p (e t)")
        wo = flat[:, 0:KD * D].rearrange("p (k n) -> p k n", k=KD)
        f = flat[:, 0:NT * D].rearrange("p (n d) -> p n d", n=NT)
        obT, oaT = sT[:, 0:CT, :], sT[:, CT:2 * CT, :]
        with nc.semaphore("const_in") as const_in, nc.Block() as block:
            @block.sync
            def _(sp):
                sp.dma_start(params[:, :], a["params"]).then_inc(const_in, 16)
                sp.dma_start(cn[:, :], a["cn"]).then_inc(const_in, 16)
                sp.wait_ge(const_in, 32)
        stages = [
            lambda: norm_to_channels(nc, a["x"], params, ident, hT),
            lambda: shifted_projection(nc, a["w_in"], params, hT, hT_dram, sT),
            lambda: scan_mixer(nc, a["lora"], params, a["cs"], ident, ones, mean, ab, sT),
            lambda: attention_projection(nc, a["w_in"], a["w_v"], hT_dram, v_dram, hT, other),
            lambda: attention(nc, a["rpb"], a["cm"], v_dram, ident, other, oaT),
            lambda: merge_branches(nc, a["w_merge"], params, hT, oaT, obT, other),
            lambda: output_projection(nc, a["x"], a["w_out"], a["gains"], params, ident, other, wo,
                                      x1_dram, hT),
            lambda: feed_forward(nc, a["w_up"], a["w_down"], a["gains"], params, hT, other, f, x1_dram, out),
            lambda: final_norm(nc, a["gains"], params, f, x1_dram, out),
        ]
        for n, s in enumerate(stages):
            if n < stop:
                s()
        if dump:
            dump(nc, locals())


def host_constants():
    import numpy as np
    eye = np.eye(P, dtype=np.float32)
    heads = np.kron(np.eye(2, dtype=np.float32), np.ones((HD, HD), np.float32))
    cn = np.concatenate([eye, heads, heads / HD], axis=1)
    reset = np.ones(T, np.float32)
    reset[::C] = 0
    keep = np.ones((2, NC), np.float32)
    keep[0, [NC_P - 1, NC - 1]] = 0
    keep[1, [0, NC_P]] = 0
    i = np.arange(P)
    s, t = i[:, None], i[None, :]
    same = (s // C) == (t // C)
    parts = [np.broadcast_to(reset, (P, T)), np.broadcast_to(keep.reshape(-1), (P, 2 * NC))]
    before = [s < t, s > t]
    for d in range(2):
        strict, incl = same & before[d], same & (before[d] | (s == t))
        parts += [strict, incl, strict, incl] if d == 0 else [incl, strict, incl, strict]
    joins = lambda d, b: (s // b == t // b) & (s // (b // 2) != t // (b // 2)) & before[d]
    for d in range(2):
        parts.append(joins(d, 2))
    for d in range(2):
        parts += [joins(d, 4 << l) for l in range(LEVELS)]
    cs = np.concatenate([np.asarray(p, np.float32) for p in parts], axis=1)
    c = np.arange(GRID_W)
    start = np.clip(c - WIN_W // 2, 0, GRID_W - WIN_W)
    ok = (c[None, :] >= start[:, None]) & (c[None, :] < start[:, None] + WIN_W)
    cm = np.tile(np.where(ok, 0.0, NEG).astype(np.float32)[::-1], (2, 1))
    return cn.astype(np.float32), np.ascontiguousarray(cs), np.ascontiguousarray(cm)


def host_layout(a):
    import numpy as np
    col = lambda v: np.asarray(v).reshape(-1, P).T
    slabs = lambda w: np.ascontiguousarray(
        w.reshape(w.shape[0] // P, P, w.shape[1] // P, P).transpose(2, 1, 0, 3)
        .reshape(w.shape[1] // P, P, w.shape[0]))
    rows = lambda w: np.ascontiguousarray(
        w.reshape(w.shape[0] // P, P, w.shape[1]).transpose(1, 0, 2))
    w_in = a["w_in"][0]
    per_pair = np.stack([col(a["w0"][0][0]), col(a["w0"][0][1]), col(a["a0"][0][0]), col(a["a0"][0][1]),
                         col(a["k_k"][0]), col(a["k_a"][0]), col(a["r_k"][0]), col(a["ln_w"][0]),
                         col(a["ln_b"][0])], axis=2).reshape(P, CT * NPC)
    eps = np.tile(np.array([[RMS_EPS, GN_EPS, KK_EPS]], np.float32), (P, 1))
    params = np.concatenate([col(a["mu_prev"][0]), col(a["mu_next"][0]), col(a["norm_pre_mix"][0]), col(a["norm_pre_ffn"][0]), per_pair, eps], axis=1)
    w2, a2, g2 = (a[n][0].reshape(P, CT, P).transpose(1, 0, 2) for n in ("w2", "a2", "g2"))
    win_t = slabs(w_in)
    merge = np.concatenate([win_t[27:35], win_t[35:43], slabs(a["w_proj_a"][0]),
                            slabs(a["w_proj_b"][0]),
                            a["b_gate"][0].reshape(2, KD, P).transpose(1, 2, 0)], axis=2)
    rp = np.zeros((8, 2 * WIN_H - 1, 2 * GRID_W - 1), np.float32)
    rp[:, :, GRID_W - WIN_W:GRID_W + WIN_W - 1] = a["rpb"][0]
    cn, cs, cm = host_constants()
    return {
        "x": np.concatenate([a["x_prompt"][0], a["x_sample"][0]], axis=0),
        "w_in": win_t[0:27], "w_v": rows(w_in[:, 1024:1536]), "w_merge": merge,
        "lora": np.stack([w2, a2, g2], axis=2), "params": params,
        "w_out": rows(a["w_out"][0]), "w_up": slabs(a["w_up"][0]),
        "w_down": a["w_down"][0].reshape(FG, FT, P, D).transpose(0, 2, 1, 3),
        "gains": np.stack([a["norm_post_mix"][0], a["norm_post_ffn"][0]]),
        "rpb": rp, "cn": cn, "cs": cs, "cm": cm,
    }


def kernel(**inputs):
    import numpy as np
    from concourse import bacc
    from concourse.bass_utils import run_bass_kernel_spmd

    laid = {n: np.ascontiguousarray(v) for n, v in
            host_layout({n: np.asarray(v) for n, v in inputs.items()}).items()}
    nc = bacc.Bacc("TRN2", target_bir_lowering=False, num_devices=1)
    args = {n: nc.dram_tensor(f"in_{n}", v.shape, mybir.dt.from_np(v.dtype), kind="ExternalInput").ap()
            for n, v in laid.items()}
    out = nc.dram_tensor("out", [T, D], F32, kind="ExternalOutput").ap()
    encoder(nc, args, out)
    got = run_bass_kernel_spmd(nc, [{f"in_{n}": v for n, v in laid.items()}], core_ids=[0]).results[0]["out"]
    return got[None, 0:TP], got[None, TP:T]
```

```python
import concourse.bass as bass
from concourse import mybir
from contextlib import ExitStack

F32 = mybir.dt.float32
ACT = mybir.ActivationFunctionType
ALU = mybir.AluOpType
AX = mybir.AxisListType

P = 128
D = 1024
KD = D // P
TP, TS = 1024, 256
T = TP + TS
NT = T // P
GROUPS = ((0, 512), (512, 512), (1024, 256))
NG = len(GROUPS)
GRID_W = 64
WIN_H, WIN_W = 8, 16
HD = 64
CT = 4
D_SH = 1920
E_SH = D_SH // P
DFF = 4096
FG = 16
FT = DFF // P // FG
C = 64
NC = T // C
NC_P = TP // C
STREAMS = 4
STEPS = 2 * NC // STREAMS
LEVELS = 5
DECAY = -0.6065306597126334
RMS_EPS, GN_EPS, KK_EPS = 1e-6, 64e-5, 1e-12
NEG = -1e30

PM_MUP, PM_MUN, PM_BG, PM_G1, PM_G2 = 0, 15, 30, 46, 54
PM_RK = 62
NPC = 9
PM_EPS = PM_RK + CT * NPC
PM_ZERO = PM_EPS + 3
PM_N = PM_ZERO + 1
(W0A, W0B, A0A, A0B, K_K, K_A, R_K, LN_W, LN_B, K_1A) = range(10)

CN_ID, CN_ONES, CN_MEAN = 0, 128, 256
CN_N = 384
CS_G = T + 2 * NC
CS_F = CS_G + 2 * 2 * P
CS_L = CS_F + 2 * P
CS_N = CS_L + 2 * LEVELS * P

E_B0, E_G0 = 12, 27
E_WL, E_AL, E_GL = 12, 13, 14


def bcast(ap, n):
    return ap.to_broadcast([ap.shape[0], n])


def split_tiles(ctx, nc, name, shape):
    return [ctx.enter_context(nc.sbuf_tensor(f"{name}{part}", shape, mybir.dt.float32r))[
        tuple(slice(None) for _ in shape)] for part in ("h", "l")]


class Steps:

    def __init__(self, eng, sem, base=0):
        self.eng, self.sem, self.base, self.n = eng, sem, base, 0

    def mark(self, ins):
        self.n += 1
        ins.then_inc(self.sem, 1)

    def wait(self):
        self.eng.wait_ge(self.sem, self.base + self.n)


def products(nc, out, stationary, moving, first, last):
    pairs = ((0, 0), (0, 1), (1, 0))
    for n, (a, b) in enumerate(pairs):
        mm = nc.tensor.matmul(out, stationary[a], moving[b], start=first and n == 0,
                              stop=last and n == len(pairs) - 1)
    return mm


def zero_like(ap, zero):
    for _ in range(len(ap.shape) - 2):
        zero = zero.unsqueeze(1)
    return zero.to_broadcast(list(ap.shape))


def split_weights(pool, nc, zero, raw, parts, loaded, high_done, split, turn, n):
    pool.wait_ge(loaded, turn * 16 + 16)
    nc.gpsimd.tensor_tensor(parts[0], raw, zero_like(raw, zero), ALU.add).then_inc(high_done, 1)
    pool.wait_ge(high_done, n + 1)
    nc.gpsimd.tensor_tensor(parts[1], raw, parts[0].bitcast(F32), ALU.subtract).then_inc(split, 1)


def norm_to_channels(nc, x, params, ident, H):
    with ExitStack() as ctx:
        sb = lambda n, s: ctx.enter_context(nc.sbuf_tensor(n, s, F32))
        sem = lambda n: ctx.enter_context(nc.semaphore(n))
        xs = [sb(f"n1_x{j}", [P, D]) for j in range(2)]
        xn = [sb(f"n1_xn{j}", [P, D]) for j in range(2)]
        sq = sb("n1_sq", [P, D])
        hb = sb("n1_h", [P, KD, P])
        st = [sb(f"n1_st{j}", [P, 3]) for j in range(2)]
        ps = [ctx.enter_context(nc.psum_tensor(f"n1_ps{j}", [P, D], F32)) for j in range(2)]
        x_in = [sem(f"n1_x_in{j}") for j in range(2)]
        sq_done, rms_ready, rstd_ready = sem("n1_sq_done"), sem("n1_rms"), sem("n1_rstd")
        xn_ready, tr_ready, h_ready = sem("n1_xn"), sem("n1_tr"), sem("n1_h")
        high, low = sem("n1_high"), sem("n1_low")
        block = ctx.enter_context(nc.Block())
        xr = x.rearrange("(n p) d -> n p d", p=P)

        @block.sync
        def _(sp):
            with sp.Fori(0, NT // 2) as i:
                for j in range(2):
                    n = i * 2 + j
                    sp.wait_ge(xn_ready, n + 1)
                    sp.dma_start(xs[j][:, :], xr[n, :, :]).then_inc(x_in[j], 16)

        @block.scalar
        def _(act):
            with act.Fori(0, NT // 2) as i:
                for j in range(2):
                    n = i * 2 + j
                    act.wait_ge(x_in[j], i * 16 + 16)
                    nc.scalar.activation(sq[:, :], xs[j][:, :], ACT.Square,
                                         accum_out=st[j][:, 0:1]).then_inc(sq_done, 1)
                    act.wait_ge(sq_done, n + 1)
                    nc.scalar.activation(st[j][:, 1:2], st[j][:, 0:1], ACT.Sqrt, scale=1.0 / D,
                                         bias=params[:, PM_EPS:PM_EPS + 1]).then_inc(rms_ready, 1)

        @block.vector
        def _(dve):
            dve.sem_inc(xn_ready, 2)
            dve.sem_inc(h_ready, 2)

            def scale(n, j):
                dve.wait_ge(rms_ready, n + 1)
                nc.vector.reciprocal(st[j][:, 2:3], st[j][:, 1:2]).then_inc(rstd_ready, 1)
                dve.wait_ge(rstd_ready, n + 1)
                dve.wait_ge(tr_ready, n + 1)
                nc.vector.tensor_scalar(xn[j][:, :], xs[j][:, :], st[j][:, 2:3], None,
                                        ALU.mult).then_inc(xn_ready, 1)

            def split(n, j):
                dve.wait_ge(tr_ready, n + 3)
                nc.vector.tensor_tensor(
                    hb[:, :, :], ps[j][:, :].rearrange("p (k t) -> p k t", k=KD),
                    params[:, PM_G1:PM_G1 + KD].unsqueeze(2).to_broadcast([P, KD, P]),
                    ALU.mult).then_inc(h_ready, 1)
                dve.wait_ge(h_ready, n + 3)
                nc.vector.tensor_copy(H[0][:, :, bass.ts(n, P)], hb[:, :, :]).then_inc(high, 1)
                dve.wait_ge(high, n + 1)
                nc.vector.tensor_tensor(H[1][:, :, bass.ts(n, P)], hb[:, :, :],
                                        H[0][:, :, bass.ts(n, P)].bitcast(F32),
                                        ALU.subtract).then_inc(low, 1)
                dve.wait_ge(low, n + 1)

            scale(0, 0)
            with dve.Fori(0, NT // 2 - 1) as i:
                for j in range(2):
                    scale(i * 2 + (j + 1), 1 - j)
                    split(i * 2 + j, j)
            scale(NT - 1, 1)
            split(NT - 2, 0)
            split(NT - 1, 1)

        @block.tensor
        def _(pe):
            pe.sem_inc(tr_ready, 2)
            with pe.Fori(0, NT // 2) as i:
                for j in range(2):
                    n = i * 2 + j
                    pe.wait_ge(xn_ready, n + 3)
                    pe.wait_ge(h_ready, n + 1)
                    for k in range(KD):
                        last = nc.tensor.transpose(ps[j][:, k * P:(k + 1) * P],
                                                   xn[j][:, k * P:(k + 1) * P], ident)
                    last.then_inc(tr_ready, 1)


def shifted_projection(nc, w_in, params, H, sT):
    with ExitStack() as ctx:
        sb = lambda n, s: ctx.enter_context(nc.sbuf_tensor(n, s, F32))
        sem = lambda n: ctx.enter_context(nc.semaphore(n))
        w = [sb(f"sp_w{j}", [P, D]) for j in range(2)]
        wp = [split_tiles(ctx, nc, f"sp_wp{j}", [P, D]) for j in range(2)]
        raw = [sb(f"sp_raw{j}", [P, T]) for j in range(2)]
        acc = [sb(f"sp_acc{j}", [P, T]) for j in range(2)]
        c0 = sb("sp_c0", [P, E_SH])
        ps = [ctx.enter_context(nc.psum_tensor(f"sp_ps{j}", [P, 1536], F32)) for j in range(2)]
        w_ld = [sem(f"sp_w_ld{j}") for j in range(2)]
        gemm, raw_ready, shifted, own_scaled, prev_added = (
            sem("sp_gemm"), sem("sp_raw"), sem("sp_shifted"), sem("sp_own"), sem("sp_prev"))
        c0_ready, lora_done, high_done, split = (
            sem("sp_c0"), sem("sp_lora"), sem("sp_high"), sem("sp_split"))
        block = ctx.enter_context(nc.Block())

        def tiles(eng, body):
            with eng.Fori(0, E_SH // 2) as i:
                for j in range(2):
                    body(i * 2 + j, j, i)
            body(E_SH - 1, 0, E_SH // 2)

        @block.sync
        def _(sp):
            def load(e, j, turn):
                sp.wait_ge(split, e + 1)
                sp.dma_start(w[j][:, :], w_in[e + E_B0, :, :]).then_inc(w_ld[j], 16)
            tiles(sp, load)

        @block.gpsimd
        def _(pool):
            pool.sem_inc(split, 2)

            def halves(e, j, turn):
                pool.wait_ge(gemm, e * NG + NG)
                split_weights(pool, nc, params[:, PM_ZERO:PM_ZERO + 1], w[j][:, :], wp[j], w_ld[j],
                              high_done, split, turn, e)
            tiles(pool, halves)

        @block.tensor
        def _(pe):
            pe.sem_inc(gemm, 2 * NG)

            def gemms(e, j, turn):
                pe.wait_ge(split, e + 3)
                for g, (t0, tn) in enumerate(GROUPS):
                    pe.wait_ge(raw_ready, e * NG + (g + 1))
                    for k in range(KD):
                        last = products(nc, ps[j][:, t0:t0 + tn], [a[:, k * P:(k + 1) * P] for a in wp[j]],
                                        [h[:, k, t0:t0 + tn] for h in H], k == 0, k == KD - 1)
                    last.then_inc(gemm, 1)
            tiles(pe, gemms)

        @block.scalar
        def _(act):
            act.sem_inc(raw_ready, 2 * NG)

            def evacuate(e, j, turn):
                act.wait_ge(shifted, e + 1)
                for g, (t0, tn) in enumerate(GROUPS):
                    act.wait_ge(gemm, e * NG + (2 * NG + g + 1))
                    nc.scalar.activation(raw[j][:, t0:t0 + tn], ps[j][:, t0:t0 + tn],
                                         ACT.Copy).then_inc(raw_ready, 1)
            tiles(act, evacuate)
            act.wait_ge(shifted, E_SH + 2)
            nc.scalar.activation(sT[:, E_WL, :], sT[:, E_WL, :], ACT.Tanh).then_inc(lora_done, 1)
            nc.scalar.activation(sT[:, E_GL, :], sT[:, E_GL, :], ACT.Sigmoid).then_inc(lora_done, 1)

        @block.vector
        def _(dve):
            dve.sem_inc(shifted, 2)
            nc.vector.tensor_tensor(c0[:, :], params[:, PM_MUP:PM_MUP + E_SH],
                                    params[:, PM_MUN:PM_MUN + E_SH], ALU.add).then_inc(c0_ready, 1)
            dve.wait_ge(c0_ready, 1)
            nc.vector.tensor_scalar(c0[:, :], c0[:, :], -1.0, 1.0, ALU.mult, ALU.add).then_inc(c0_ready, 1)
            dve.wait_ge(c0_ready, 2)

            def shift(e, j, turn):
                dve.wait_ge(raw_ready, e * NG + 3 * NG)
                nc.vector.tensor_scalar(acc[j][:, :], raw[j][:, :], c0[:, bass.ds(e, 1)], None,
                                        ALU.mult).then_inc(own_scaled, 1)
                dve.wait_ge(own_scaled, e + 1)
                for lo, hi in ((1, TP), (TP + 1, T)):
                    nc.vector.scalar_tensor_tensor(
                        acc[j][:, lo:hi], raw[j][:, lo - 1:hi - 1],
                        params[:, bass.ds(e + PM_MUP, 1)], acc[j][:, lo:hi],
                        ALU.mult, ALU.add).then_inc(prev_added, 1)
                dve.wait_ge(prev_added, e * 2 + 2)
                for lo, hi in ((0, TP - 1), (TP, T - 1)):
                    nc.vector.scalar_tensor_tensor(
                        sT[:, bass.ds(e, 1), lo:hi], raw[j][:, lo + 1:hi + 1],
                        params[:, bass.ds(e + PM_MUN, 1)], acc[j][:, lo:hi], ALU.mult, ALU.add)
                nc.vector.tensor_copy(sT[:, bass.ds(e, 1), TP - 1:T:TS], acc[j][:, TP - 1:T:TS]
                                      ).then_inc(shifted, 1)
            tiles(dve, shift)
            dve.wait_ge(shifted, E_SH + 2)


def scan_mixer(nc, lora, params, cn_scan, ident, ones, mean, ab, sT):
    with ExitStack() as ctx:
        sb = lambda n, s: ctx.enter_context(nc.sbuf_tensor(n, s, F32))
        sems = []

        def sem(n):
            sems.append(nc.alloc_semaphore("sc_" + n))
            return sems[-1]

        AR = ab[:, 0:9 * T].rearrange("p (n t) -> p n t", t=T)
        AX_ = [dict(a=0, r=1, b=2, k=3), dict(k=5, b=6, r=7, a=8)]
        V = 4
        kk, lw, cum, neg, icl, kds = (ab[:, (9 + n) * T:(10 + n) * T] for n in range(6))
        norm = AR[:, AX_[1]["a"], :]
        y = [lw, cum]
        wl = sb("sc_lora", [P, 3, P])
        pc = sb("sc_pc", [P, NPC + 1])
        edge = sb("sc_edge", [P, 2, NC])
        cs = sb("sc_cs", [P, CS_N])
        reset, keep = cs[:, 0:T], cs[:, T:T + 2 * NC].rearrange("p (d c) -> p d c", d=2)
        gmask = [cs[:, CS_G + d * 2 * P:CS_G + (d + 1) * 2 * P].unsqueeze(1).to_broadcast([P, 2, 2 * P])
                 for d in range(2)]
        first = [cs[:, CS_F + d * P:CS_F + (d + 1) * P] for d in range(2)]
        lmask = [cs[:, CS_L + d * LEVELS * P:CS_L + (d + 1) * LEVELS * P]
                 .rearrange("p (l t) -> p l t", l=LEVELS) for d in range(2)]
        BD = [sb(f"sc_bd{s}", [P, 6, P]) for s in range(STREAMS - 1)]
        BD.append(ab[:, 15 * T:15 * T + 6 * P].rearrange("p (n t) -> p n t", t=P))
        BX = [dict(a=1, r=2, b=3, k=4, v=5), dict(v=1, k=2, b=3, r=4, a=5)] * 2
        WK = [sb(f"sc_wk{s}", [P, 11, P]) for s in range(STREAMS)]
        GX = [dict(ab=5, rb=6, ak=7, rk=8), dict(rb=5, ab=6, rk=7, ak=8)] * 2
        free_k = kk.rearrange("p (n t) -> p n t", t=P)
        free_i = icl.rearrange("p (n t) -> p n t", t=P)
        free_n = neg.rearrange("p (n t) -> p n t", t=P)
        ML = [f[:, LEVELS * i:LEVELS * (i + 1), :] for f in (free_n, free_k) for i in range(2)]
        MR = [m[:, LEVELS - 2:LEVELS, :] for m in ML]
        XY = ([sb(f"sc_xy{s}", [P, 2, P]) for s in range(2)]
              + [free_i[:, 2 * s:2 * s + 2, :] for s in range(2)])
        Q1 = ([sb(f"sc_q{s}", [P, P]) for s in range(2)] + [free_i[:, 4 + s, :] for s in range(2)])
        S = [sb(f"sc_s{d}", [P, P]) for d in range(2)]
        ps = ctx.enter_context(nc.psum_tensor("sc_ps", [P, 8, 512], F32))
        bankA, bankB = ([ps[:, 2 * s + i, :] for s in range(STREAMS)] for i in range(2))
        psA = ps[:, 0:3, :].rearrange("p b n -> p (b n)")
        psB = ps[:, 4:7, :].rearrange("p b n -> p (b n)")

        cs_in, zeroed, lora_in = sem("cs_in"), sem("zeroed"), sem("lora_in")
        pc_ready, sq_ready, ss_ps, nrm_ready, kk_ready = (
            sem("pc"), sem("sq"), sem("ss_ps"), sem("nrm"), sem("kk"))
        zw_ps, za_ps, sg_ready, icl_ready, cum_ready, exps_ready, arr_ready = (
            sem("zw_ps"), sem("za_ps"), sem("sg"), sem("icl"), sem("cum"), sem("exps"), sem("arr"))
        v_ready, b_ready, kp_ready, kds_ready, lw_used, rk_ready, fac_ready = (
            sem("v"), sem("b"), sem("kp"), sem("kds"), sem("lw_used"), sem("rk"),
            sem("fac"))
        dch, pdone = sem("dch"), sem("pair_done")
        ysum, mean_ps, yc_ready, ysq, var_ps, std_ready, gb_ps = (
            sem("ysum"), sem("mean_ps"), sem("yc"), sem("ysq"), sem("var_ps"), sem("std"),
            sem("gb_ps"))
        bd_ready, bd_ready2, gram, bytok, masked, copied = (
            sem("bd"), sem("bd2"), sem("gram"), sem("bytok"), sem("masked"), sem("copied"))
        lvl0_ready, lvl_ready, y1_ready, y1h, x1t, x1c = (
            sem("lvl0"), sem("lvl"), sem("y1"), sem("y1h"), sem("x1t"), sem("x1c"))
        q_ps, q_ready, xy_ps, xy_ready = sem("q_ps"), sem("q"), sem("xy_ps"), sem("xy")
        w1_ps, w1_ready, u_ps, u_ready = sem("w1_ps"), sem("w1"), sem("u_ps"), sem("u")
        m_ps, m_ready, s_ps, s_ready, y_ready = (
            sem("m_ps"), sem("m"), sem("s_ps"), sem("s"), sem("y"))
        NZ = 2 * STREAMS + 2
        NDCH = 7
        block = ctx.enter_context(nc.Block())

        def chunk_of(s, j):
            return j * 2 + s // 2 if s % 2 == 0 else j * -2 + (NC - 1 - s // 2)

        def nth(q, s):
            return q * STREAMS + (s + 1)

        def nth_level(q, l, s):
            return q * (LEVELS * STREAMS) + (l * STREAMS + s + 1)

        @block.sync
        def _(sp):
            sp.dma_start(cs[:, :], cn_scan).then_inc(cs_in, 16)
            with sp.Fori(0, CT) as ct:
                sp.wait_ge(pdone, ct + 1)
                sp.dma_start(wl[:, :, :], lora[ct, :, :, :]).then_inc(lora_in, 16)

        @block.gpsimd
        def _(pool):
            for s in range(STREAMS):
                nc.gpsimd.memset(BD[s][:, 1:6, :], 0.0).then_inc(zeroed, 1)
                nc.gpsimd.tensor_copy(BD[s][:, 0, :], ident).then_inc(zeroed, 1)
            for d in range(2):
                nc.gpsimd.memset(S[d][:, :], 0.0).then_inc(zeroed, 1)
            pool.wait_ge(zeroed, NZ)
            pool.wait_ge(cs_in, 16)
            with pool.Fori(0, CT) as ct:
                pool.wait_ge(pdone, ct + 1)
                nc.gpsimd.tensor_copy(AR[:, V, :], sT[:, bass.ds(ct + 8, 1), :]).then_inc(v_ready, 1)
                for d in range(2):
                    x = AX_[d]
                    pool.wait_ge(kk_ready, ct + 1)
                    pool.wait_ge(icl_ready, ct * 2 + (d + 1))
                    nc.gpsimd.tensor_tensor(AR[:, x["b"], :], kk, icl, ALU.mult).then_inc(b_ready, 1)
                    pool.wait_ge(kp_ready, ct * 2 + (d + 1))
                    nc.gpsimd.tensor_tensor(kds, AR[:, x["k"], :],
                                            zero_like(AR[:, x["k"], :], params[:, PM_ZERO:PM_ZERO + 1])
                                            if d == 0 else kds, ALU.add).then_inc(kds_ready, 1)
                    if d == 0:
                        pool.wait_ge(kds_ready, ct * 2 + 1)
                with pool.Fori(0, STEPS) as j:
                    q = ct * STEPS + j
                    pool.wait_ge(kds_ready, ct * 2 + 2)
                    pool.wait_ge(v_ready, ct + 1)
                    pool.wait_ge(arr_ready, ct * 2 + 2)
                    for s in range(STREAMS):
                        pool.wait_ge(m_ready, nth(q, s))
                        lo = 4 * (s % 2)
                        nc.gpsimd.tensor_copy(BD[s][C:P, 1:6, C:P],
                                              AR[C:P, lo:lo + 5, bass.ts(chunk_of(s, j), C)]
                                              ).then_inc(bd_ready2, 1)
                    pool.wait_ge(bd_ready2, nth(q, STREAMS - 1))
                    for l0, l1, ready in ((0, 1, lvl0_ready), (1, LEVELS, lvl_ready)):
                        for s in range(STREAMS):
                            pool.wait_ge(masked, nth(q, s))
                            nc.gpsimd.tensor_tensor(
                                ML[s][:, l0:l1, :],
                                WK[s][:, GX[s]["ab"], :].unsqueeze(1).to_broadcast([P, l1 - l0, P]),
                                lmask[s % 2][:, l0:l1, :], ALU.mult).then_inc(ready, 1)

        @block.tensor
        def _(pe):
            def over_tokens(dst, lhsT, rhs):
                for t0, tn in GROUPS:
                    last = nc.tensor.matmul(dst[:, t0:t0 + tn], lhsT, rhs[:, t0:t0 + tn],
                                            start=True, stop=True)
                return last

            pe.wait_ge(zeroed, NZ)
            with pe.Fori(0, CT) as ct:
                pe.wait_ge(lora_in, ct * 16 + 16)
                pe.wait_ge(sq_ready, ct + 1)
                over_tokens(psA, ones, neg).then_inc(ss_ps, 1)
                for d in range(2):
                    rows = slice(d * HD, (d + 1) * HD)
                    if d:
                        pe.wait_ge(sg_ready, ct * 2 + 1)
                    over_tokens(psB, wl[rows, 0, :], sT[rows, E_WL, :]).then_inc(zw_ps, 1)
                    if d:
                        pe.wait_ge(icl_ready, ct * 2 + 1)
                    else:
                        pe.wait_ge(nrm_ready, ct + 1)
                    over_tokens(psA, wl[rows, 1, :], sT[rows, E_AL, :]).then_inc(za_ps, 1)

                with pe.Fori(0, STEPS) as j:
                    q = ct * STEPS + j
                    pe.wait_ge(arr_ready, ct * 2 + 2)
                    for s in range(STREAMS):
                        pe.wait_ge(bd_ready, nth(q, s))
                        pe.wait_ge(bd_ready2, nth(q, s))
                        pe.wait_ge(y_ready, nth(q, s))
                        x = BX[s]
                        lo = min(x["a"], x["r"])
                        rhs = BD[s][:, lo:lo + 2, :]
                        nc.tensor.matmul(bankA[s][:, 0:256], BD[s][:, x["b"], :], rhs,
                                         start=True, stop=True)
                        nc.tensor.matmul(bankA[s][:, 256:512], BD[s][:, x["k"], :], rhs,
                                         start=True, stop=True).then_inc(gram, 1)
                        pe.wait_ge(s_ready, nth(q, s))
                        for n, name in enumerate("abkv"):
                            last = nc.tensor.transpose(bankB[s][:, n * P:(n + 1) * P],
                                                       BD[s][:, x[name], :], ident)
                        last.then_inc(bytok, 1)
                    for s in range(STREAMS):
                        pe.wait_ge(copied, nth(q, s))
                        pe.wait_ge(y1_ready, nth(q, s))
                        nc.tensor.transpose(bankB[s][:, 3 * P:4 * P], XY[s][:, 1, :], ident
                                            ).then_inc(x1t, 1)
                    for l in range(LEVELS):
                        for s in range(STREAMS):
                            if l == 0:
                                pe.wait_ge(lvl0_ready, nth(q, s))
                                pe.wait_ge(x1c, nth(q, s))
                            else:
                                pe.wait_ge(xy_ready, nth_level(q, l - 1, s))
                            if l == 1:
                                pe.wait_ge(lvl_ready, nth(q, s))
                            nc.tensor.matmul(bankB[s][:, 0:P], ML[s][:, l, :], XY[s][:, 0, :],
                                             start=True, stop=True).then_inc(q_ps, 1)
                        if l == 0:
                            for s in range(STREAMS):
                                nc.tensor.matmul(bankA[s][:, 0:P], WK[s][:, GX[s]["ak"], :],
                                                 WK[s][:, 3, :], start=True, stop=True
                                                 ).then_inc(w1_ps, 1)
                        for s in range(STREAMS):
                            pe.wait_ge(q_ready, nth_level(q, l, s))
                            if l < LEVELS - 1:
                                nc.tensor.matmul(bankB[s][:, P:2 * P], XY[s][:, 1, :],
                                                 Q1[s][:, :], start=True, stop=True)
                            nc.tensor.matmul(bankB[s][:, 2 * P:3 * P], Q1[s][:, :],
                                             XY[s][:, 1, :], start=True, stop=True
                                             ).then_inc(xy_ps, 1)
                    for s in range(STREAMS):
                        pe.wait_ge(w1_ready, nth(q, s))
                        pe.wait_ge(xy_ready, nth_level(q, LEVELS - 1, s))
                        nc.tensor.matmul(bankA[s][:, P:3 * P], XY[s][:, 1, :],
                                         WK[s][:, 0:5:4, :], start=True, stop=True
                                         ).then_inc(u_ps, 1)
                    for s in range(STREAMS):
                        rb = GX[s]["rb"]
                        pe.wait_ge(u_ready, nth(q, s))
                        nc.tensor.matmul(bankA[s][:, 0:256], WK[s][:, 9, :],
                                         WK[s][:, 1:rb + 1:rb - 1, :], start=True, stop=True
                                         ).then_inc(m_ps, 1)
                    for s in range(STREAMS):
                        g = GX[s]
                        yp, sp_ = bankA[s][:, 3 * P:4 * P], bankB[s][:, 0:P]
                        nc.tensor.matmul(sp_, WK[s][:, 1, :], WK[s][:, 10, :], start=True, stop=False)
                        nc.tensor.matmul(sp_, WK[s][:, 2, :], WK[s][:, 3, :], start=False, stop=False)
                        pe.wait_ge(m_ready, nth(q, s) + STREAMS)
                        nc.tensor.matmul(yp, WK[s][:, 10, :], WK[s][:, g["rb"], :], start=True, stop=False)
                        nc.tensor.matmul(yp, WK[s][:, 3, :], WK[s][:, g["rk"], :], start=False, stop=False)
                        pe.wait_ge(s_ready, nth(q, s) + (STREAMS - 2))
                        nc.tensor.matmul(yp, S[s % 2][:, :], MR[s][:, 1, :], start=False, stop=True)
                        nc.tensor.matmul(sp_, MR[s][:, 0, :], S[s % 2][:, :], start=False, stop=True
                                         ).then_inc(s_ps, 1)

                pe.wait_ge(ysum, ct + 1)
                over_tokens(psA, mean, lw).then_inc(mean_ps, 1)
                pe.wait_ge(ysq, ct + 1)
                over_tokens(psB, mean, neg).then_inc(var_ps, 1)
                pe.wait_ge(rk_ready, ct + 1)
                pe.wait_ge(std_ready, ct + 1)
                over_tokens(psA, ones, kds)
                over_tokens(psB, wl[:, 2, :], sT[:, E_GL, :]).then_inc(gb_ps, 1)

        @block.scalar
        def _(act):
            with act.Fori(0, CT) as ct:
                k = sT[:, bass.ds(ct + 4, 1), :]
                act.wait_ge(pc_ready, ct * 2 + 2)
                nc.scalar.activation(neg, k, ACT.Square, scale=pc[:, K_K:K_K + 1]).then_inc(sq_ready, 1)
                nc.scalar.activation(kk, k, ACT.Copy, scale=pc[:, K_K:K_K + 1])
                act.wait_ge(ss_ps, ct + 1)
                nc.scalar.activation(norm, psA[:, 0:T], ACT.Sqrt,
                                     bias=params[:, PM_EPS + 2:PM_EPS + 3]).then_inc(nrm_ready, 1)
                for d in range(2):
                    act.wait_ge(zw_ps, ct * 2 + (d + 1))
                    if d:
                        act.wait_ge(lw_used, ct * 2 + 1)
                    nc.scalar.activation(lw, psB[:, 0:T], ACT.Sigmoid,
                                         bias=pc[:, W0A + d:W0A + d + 1]).then_inc(sg_ready, 1)
                    act.wait_ge(za_ps, ct * 2 + (d + 1))
                    if d:
                        act.wait_ge(b_ready, ct * 2 + 1)
                    nc.scalar.activation(icl, psA[:, 0:T], ACT.Sigmoid,
                                         bias=pc[:, A0A + d:A0A + d + 1]).then_inc(icl_ready, 1)
                    act.wait_ge(icl_ready, ct * 2 + (d + 1))
                    nc.scalar.activation(AR[:, AX_[d]["k"], :], icl, ACT.Identity, scale=pc[:, K_A:K_A + 1],
                                         bias=pc[:, K_1A:K_1A + 1]).then_inc(fac_ready, 1)
                    act.wait_ge(cum_ready, ct * 2 + (d + 1))
                    nc.scalar.activation(neg, cum, ACT.Exp, scale=-DECAY)
                    nc.scalar.activation(lw, lw, ACT.Exp, scale=DECAY)
                    nc.scalar.activation(cum, cum, ACT.Exp, scale=DECAY).then_inc(exps_ready, 1)

                with act.Fori(0, STEPS) as j:
                    q = ct * STEPS + j
                    act.wait_ge(arr_ready, ct * 2 + 2)
                    for s in range(STREAMS):
                        act.wait_ge(m_ready, nth(q, s))
                        lo = 4 * (s % 2)
                        nc.scalar.activation(BD[s][0:C, 1:6, 0:C],
                                             AR[0:C, lo:lo + 5, bass.ts(chunk_of(s, j), C)],
                                             ACT.Copy).then_inc(bd_ready, 1)
                    for s in range(STREAMS):
                        act.wait_ge(bytok, nth(q, s))
                        nc.scalar.activation(WK[s][:, 0:4, :], bankB[s], ACT.Copy
                                             ).then_inc(copied, 1)
                    for s in range(STREAMS):
                        act.wait_ge(x1t, nth(q, s))
                        nc.scalar.activation(XY[s][:, 0, :], bankB[s][:, 3 * P:4 * P], ACT.Copy
                                             ).then_inc(x1c, 1)
                    for l in range(LEVELS):
                        for s in range(STREAMS):
                            act.wait_ge(xy_ps, nth_level(q, l, s))
                            h = 0 if l < LEVELS - 1 else 1
                            nc.scalar.activation(XY[s][:, h:2, :],
                                                 bankB[s][:, (1 + h) * P:3 * P], ACT.Copy
                                                 ).then_inc(xy_ready, 1)
                    for s in range(STREAMS):
                        act.wait_ge(u_ps, nth(q, s))
                        nc.scalar.activation(WK[s][:, 9:11, :], bankA[s][:, P:3 * P], ACT.Copy
                                             ).then_inc(u_ready, 1)

                act.wait_ge(yc_ready, ct + 1)
                nc.scalar.activation(neg, lw, ACT.Square).then_inc(ysq, 1)
                act.wait_ge(var_ps, ct + 1)
                nc.scalar.activation(cum, psB[:, 0:T], ACT.Sqrt,
                                     bias=params[:, PM_EPS + 1:PM_EPS + 2]).then_inc(std_ready, 1)

        @block.vector
        def _(dve):
            for sem_ in (m_ready, s_ready, y_ready):
                dve.sem_inc(sem_, STREAMS)
            dve.sem_inc(pdone, 1)
            dve.wait_ge(cs_in, 16)
            dve.wait_ge(zeroed, NZ)
            with dve.Fori(0, CT) as ct:
                own = Steps(dve, dch, ct * NDCH)
                r, k, v = (sT[:, bass.ds(ct + 4 * n, 1), :] for n in range(3))
                nc.vector.tensor_copy(pc[:, 0:NPC], params[:, bass.ds(ct * NPC + PM_RK, NPC)]
                                      ).then_inc(pc_ready, 1)
                dve.wait_ge(pc_ready, ct * 2 + 1)
                nc.vector.tensor_scalar(pc[:, K_1A:K_1A + 1], pc[:, K_A:K_A + 1], -1.0, 1.0,
                                        ALU.mult, ALU.add).then_inc(pc_ready, 1)
                for d in range(2):
                    x = AX_[d]
                    way = slice(None) if d == 0 else slice(None, None, -1)
                    if d:
                        dve.wait_ge(arr_ready, ct * 2 + 1)
                    dve.wait_ge(sg_ready, ct * 2 + (d + 1))
                    own.mark(nc.vector.tensor_tensor_scan(cum[:, way], reset, lw[:, way], 0.0,
                                                          ALU.mult, ALU.add))
                    own.wait()
                    nc.vector.tensor_tensor(lw, cum, lw, ALU.subtract).then_inc(cum_ready, 1)
                    if d == 0:
                        dve.wait_ge(nrm_ready, ct + 1)
                        own.mark(nc.vector.reciprocal(norm, norm))
                        own.wait()
                        nc.vector.tensor_tensor(kk, kk, norm, ALU.mult).then_inc(kk_ready, 1)
                    dve.wait_ge(fac_ready, ct * 2 + (d + 1))
                    nc.vector.tensor_tensor(AR[:, x["k"], :], AR[:, x["k"], :], k, ALU.mult
                                            ).then_inc(kp_ready, 1)
                    dve.wait_ge(kk_ready, ct + 1)
                    dve.wait_ge(exps_ready, ct * 2 + (d + 1))
                    nc.vector.scalar_tensor_tensor(AR[:, x["a"], :], kk, -1.0, lw, ALU.mult, ALU.mult
                                                   ).then_inc(lw_used, 1)
                    nc.vector.tensor_tensor(AR[:, x["r"], :], r, cum, ALU.mult)
                    at = C - 1 if d == 0 else 0
                    nc.vector.tensor_tensor(edge[:, d, :], cum[:, at:T:C], keep[:, d, :], ALU.mult)
                    dve.wait_ge(b_ready, ct * 2 + (d + 1))
                    nc.vector.tensor_tensor(AR[:, x["b"], :], AR[:, x["b"], :], neg, ALU.mult)
                    dve.wait_ge(kds_ready, ct * 2 + (d + 1))
                    nc.vector.tensor_tensor(AR[:, x["k"], :], AR[:, x["k"], :], neg, ALU.mult
                                            ).then_inc(arr_ready, 1)

                with dve.Fori(0, STEPS) as j:
                    q = ct * STEPS + j
                    for s in range(STREAMS + 1):
                        if s < STREAMS:
                            dve.wait_ge(gram, nth(q, s))
                            nc.vector.tensor_tensor(
                                WK[s][:, 5:9, :].rearrange("p (n m) t -> p n (m t)", n=2),
                                bankA[s].rearrange("p (n t) -> p n t", n=2), gmask[s % 2], ALU.mult
                            ).then_inc(masked, 1)
                        if s >= 1:
                            h = s - 1
                            dve.wait_ge(masked, nth(q, h))
                            nc.vector.tensor_tensor(XY[h][:, 1, :], WK[h][:, GX[h]["ab"], :],
                                                    first[h % 2], ALU.mult).then_inc(y1h, 1)
                            dve.wait_ge(y1h, nth(q, h))
                            nc.vector.tensor_tensor(XY[h][:, 1, :], XY[h][:, 1, :], ident, ALU.add
                                                    ).then_inc(y1_ready, 1)
                    for l in range(LEVELS):
                        for s in range(STREAMS):
                            dve.wait_ge(q_ps, nth_level(q, l, s))
                            nc.vector.tensor_tensor(Q1[s][:, :], bankB[s][:, 0:P], ident, ALU.add
                                                    ).then_inc(q_ready, 1)
                        if l == 0:
                            for s in range(STREAMS):
                                dve.wait_ge(w1_ps, nth(q, s))
                                nc.vector.tensor_copy(WK[s][:, 4, :], bankA[s][:, 0:P]
                                                      ).then_inc(w1_ready, 1)
                    for s in range(STREAMS):
                        r_ = BX[s]["r"]
                        dve.wait_ge(m_ps, nth(q, s))
                        nc.vector.tensor_tensor(MR[s], bankA[s][:, 0:256],
                                                BD[s][:, 0:r_ + 1:r_, :], ALU.add
                                                ).then_inc(m_ready, 1)
                    for s in range(STREAMS):
                        d, c = s % 2, chunk_of(s, j)
                        dve.wait_ge(s_ps, nth(q, s))
                        nc.vector.tensor_scalar(S[d][:, :], bankB[s][:, 0:P],
                                                edge[:, d, bass.ds(c, 1)], None, ALU.mult
                                                ).then_inc(s_ready, 1)
                        nc.vector.tensor_reduce(
                            y[d][:, bass.ts(c, C)],
                            bankA[s][:, 3 * P:4 * P].rearrange("p (h t) -> p t h", h=2),
                            AX.X, ALU.add).then_inc(y_ready, 1)

                dve.wait_ge(y_ready, ct * (STEPS * STREAMS) + (STEPS + 1) * STREAMS)
                nc.vector.tensor_tensor(lw, lw, cum, ALU.add).then_inc(ysum, 1)
                dve.wait_ge(mean_ps, ct + 1)
                nc.vector.tensor_tensor(lw, lw, psA[:, 0:T], ALU.subtract).then_inc(yc_ready, 1)
                nc.vector.scalar_tensor_tensor(kds, r, pc[:, R_K:R_K + 1], kds, ALU.mult, ALU.mult
                                               ).then_inc(rk_ready, 1)
                dve.wait_ge(std_ready, ct + 1)
                own.mark(nc.vector.reciprocal(cum, cum))
                own.wait()
                own.mark(nc.vector.tensor_tensor(lw, lw, cum, ALU.mult))
                dve.wait_ge(gb_ps, ct + 1)
                own.mark(nc.vector.tensor_tensor(icl, v, psA[:, 0:T], ALU.mult))
                own.wait()
                own.mark(nc.vector.scalar_tensor_tensor(icl, lw, pc[:, LN_W:LN_W + 1], icl,
                                                        ALU.mult, ALU.add))
                own.wait()
                nc.vector.scalar_tensor_tensor(r, icl, pc[:, LN_B:LN_B + 1], psB[:, 0:T],
                                               ALU.add, ALU.mult).then_inc(pdone, 1)
                assert own.n == NDCH, own.n
                dve.wait_ge(pdone, ct + 2)

    nc.clear_and_free_semaphores(sems)
    nc.all_engine_barrier()


def attention_projection(nc, params, w_in, w_v, v_dram, H, qk):
    E_QK, HV = 2 * CT, 256
    with ExitStack() as ctx:
        zero = params[:, PM_ZERO:PM_ZERO + 1]
        sb = lambda n, s: ctx.enter_context(nc.sbuf_tensor(n, s, F32))
        sem = lambda n: ctx.enter_context(nc.semaphore("ap_" + n))
        w = sb("ap_w", [P, 2, D])
        wp = split_tiles(ctx, nc, "ap_wp", [P, 2, D])
        wv = [a.rearrange("p j (k n) -> p (j k) n", n=HV) for a in wp]
        vt = [sb(f"ap_vt{j}", [P, HV]) for j in range(2)]
        ps = [ctx.enter_context(nc.psum_tensor(f"ap_ps{j}", [P, 1536], F32)) for j in range(2)]
        pv = [ctx.enter_context(nc.psum_tensor(f"ap_pv{j}", [P, 512], F32)) for j in range(2)]
        w_ld = [sem(f"w_ld{j}") for j in range(2)]
        v_out = [sem(f"v_out{j}") for j in range(2)]
        wv_in, gemm, qk_ready, v_ps, v_ready, high_done, split, stored = (
            sem("wv_in"), sem("gemm"), sem("qk"), sem("v_ps"), sem("v"), sem("high"), sem("split"),
            sem("stored"))
        block = ctx.enter_context(nc.Block())

        @block.sync
        def _(sp):
            with sp.Fori(0, E_QK // 2) as i:
                for j in range(2):
                    e = i * 2 + j
                    sp.wait_ge(split, e + 1)
                    sp.dma_start(w[:, j, :], w_in[e, :, :]).then_inc(w_ld[j], 16)
            with sp.Fori(0, 2) as hv:
                sp.wait_ge(split, hv + (E_QK + 2))
                sp.dma_start(w[:, :, :].rearrange("p j n -> p (j n)"), w_v[hv, :, :]).then_inc(wv_in, 16)

        @block.gpsimd
        def _(pool):
            pool.sem_inc(split, 2)
            pool.sem_inc(stored, 2)
            with pool.Fori(0, E_QK // 2) as i:
                for j in range(2):
                    e = i * 2 + j
                    pool.wait_ge(gemm, e * NG + NG)
                    split_weights(pool, nc, zero, w[:, j, :], [a[:, j, :] for a in wp], w_ld[j],
                                  high_done, split, i, e)
            with pool.Fori(0, 2) as hv:
                pool.wait_ge(gemm, E_QK * NG + 2 * NG)
                pool.wait_ge(v_ps, hv * NT + 1)
                split_weights(pool, nc, zero, w[:, :, :], wp, wv_in, high_done, split, hv, hv + E_QK)
                for n in range(NT):
                    pool.wait_ge(v_ready, hv * NT + (n + 3))
                    pool.dma_start(v_dram[n * P:(n + 1) * P, bass.ts(hv, HV)], vt[n % 2][:, :]
                                   ).then_inc(v_out[n % 2], 16)
                    pool.wait_ge(v_out[n % 2], hv * (NT // 2 * 16) + (n // 2 + 1) * 16)
                    pool.sem_inc(stored, 1)

        @block.tensor
        def _(pe):
            pe.sem_inc(gemm, 2 * NG)
            pe.sem_inc(v_ps, 1)
            with pe.Fori(0, E_QK // 2) as i:
                for j in range(2):
                    e = i * 2 + j
                    pe.wait_ge(split, e + 3)
                    for g, (t0, tn) in enumerate(GROUPS):
                        pe.wait_ge(qk_ready, e * NG + (g + 1))
                        for k in range(KD):
                            last = products(nc, ps[j][:, t0:t0 + tn],
                                            [a[:, j, k * P:(k + 1) * P] for a in wp],
                                            [h[:, k, t0:t0 + tn] for h in H], k == 0, k == KD - 1)
                        last.then_inc(gemm, 1)
            with pe.Fori(0, 2) as hv:
                pe.wait_ge(split, hv + (E_QK + 3))
                for n in range(NT):
                    pe.wait_ge(v_ready, hv * NT + (n + 1))
                    for k in range(KD):
                        last = products(nc, pv[n % 2][:, 0:HV], [h[:, k, n * P:(n + 1) * P] for h in H],
                                        [a[:, k, :] for a in wv], k == 0, k == KD - 1)
                    last.then_inc(v_ps, 1)

        @block.scalar
        def _(act):
            act.sem_inc(qk_ready, 2 * NG)
            with act.Fori(0, E_QK // 2) as i:
                for j in range(2):
                    e = i * 2 + j
                    for g, (t0, tn) in enumerate(GROUPS):
                        act.wait_ge(gemm, e * NG + (2 * NG + g + 1))
                        nc.scalar.activation(qk[:, bass.ds(e, 1), t0:t0 + tn], ps[j][:, t0:t0 + tn],
                                             ACT.Copy).then_inc(qk_ready, 1)
            act.wait_ge(qk_ready, E_QK * NG + 2 * NG)

        @block.vector
        def _(dve):
            dve.sem_inc(v_ready, 2)
            with dve.Fori(0, 2) as hv:
                for n in range(NT):
                    dve.wait_ge(stored, hv * NT + (n + 1))
                    dve.wait_ge(v_ps, hv * NT + (n + 2))
                    nc.vector.tensor_copy(vt[n % 2][:, :], pv[n % 2][:, 0:HV]).then_inc(v_ready, 1)


def attention(nc, rpb, cm, v_dram, oa_dram, ident, qk, oT):
    ROWS = []
    for base, tokens in ((0, TP), (TP, TS)):
        rows = tokens // GRID_W
        kh = min(WIN_H, rows)
        for r in range(rows):
            r0 = min(max(r - kh // 2, 0), rows - kh)
            ROWS.append((base + r * GRID_W, base + r0 * GRID_W, kh * GRID_W, r0 - r + WIN_H - 1))
    NR, NDR = len(ROWS), 2 * WIN_H - 1
    NB = 4
    assert NR % NB == 0
    NODD = (TP - GRID_W) // P

    def backwards(h):
        return slice(h * GRID_W + GRID_W - 1, h * GRID_W - 1 if h else None, -1)

    with ExitStack() as ctx:
        sb = lambda n, s: ctx.enter_context(nc.sbuf_tensor(n, s, F32))
        sem = lambda n: ctx.enter_context(nc.semaphore("at_" + n))
        bias = sb("at_bias", [P, CT, NDR * GRID_W])
        cms = sb("at_cm", [P, GRID_W])
        v_even, v_odd = sb("at_ve", [P, NT, P]), sb("at_vo", [P, NODD, P])
        qb = [sb(f"at_qb{j}", [P, P]) for j in range(2)]
        sc = [sb(f"at_sc{j}", [P, 512]) for j in range(NB)]
        pr = [sb(f"at_pr{j}", [P, 512]) for j in range(NB)]
        prT = [sb(f"at_prT{j}", [P, 512]) for j in range(2)]
        st = [sb(f"at_st{j}", [P, 4]) for j in range(NB)]
        pb = lambda n: [ctx.enter_context(nc.psum_tensor(f"at_{n}{j}", [P, 512], F32)) for j in range(2)]
        s_ps, t_ps, o_ps = pb("s"), pb("t"), pb("o")
        bias_in, bias_ready, zeroed, v_in = sem("bias_in"), sem("bias"), sem("zeroed"), sem("v_in")
        q_ready, scores, biased, maxed, shift_ready, exped, summed, normed = (
            sem("q"), sem("scores"), sem("biased"), sem("maxed"), sem("shift"), sem("exp"),
            sem("sum"), sem("norm"))
        turned, turned_c, pv_done, o_ready = sem("turned"), sem("turned_c"), sem("pv"), sem("o")
        o_out = sem("o_out")
        block = ctx.enter_context(nc.Block())

        @block.sync
        def _(sp):
            with nc.allow_non_contiguous_dma(reason="v tiles of a head pair"):
                with sp.Fori(0, CT) as p:
                    sp.wait_ge(pv_done, p * NR + 2)
                    sp.dma_start(v_even[:, :, :], v_dram.rearrange("(n p) c -> p n c", p=P)
                                 [:, :, bass.ts(p, P)]).then_inc(v_in, 16)
                    sp.dma_start(v_odd[:, :, :], v_dram[GRID_W:GRID_W + NODD * P, :]
                                 .rearrange("(n p) c -> p n c", p=P)[:, :, bass.ts(p, P)]
                                 ).then_inc(v_in, 16)
            sp.wait_ge(o_ready, CT * NR + 2)
            sp.dma_start(oa_dram, oT).then_inc(o_out, 16)
            sp.wait_ge(o_out, 16)

        @block.gpsimd
        def _(pool):
            for j in range(2):
                nc.gpsimd.memset(qb[j][:, :], 0.0).then_inc(zeroed, 1)
            pool.wait_ge(zeroed, 2)
            with pool.Fori(0, CT) as p:
                for r, (q0, k0, nk, dr) in enumerate(ROWS):
                    n, j = p * NR + r, r % 2
                    pool.wait_ge(scores, n + 1)
                    for h in range(2):
                        rows = slice(h * HD, (h + 1) * HD)
                        nc.gpsimd.tensor_copy(qb[j][rows, backwards(h)],
                                              qk[rows, bass.ds(p, 1), q0:q0 + GRID_W]
                                              ).then_inc(q_ready, 1)

        @block.tensor
        def _(pe):
            pe.sem_inc(scores, 2)
            pe.sem_inc(turned, NB)
            pe.sem_inc(pv_done, 2)
            with pe.Fori(0, CT) as p:
                for step in range(NR + 3):
                    if step < NR:
                        q0, k0, nk, dr = ROWS[step]
                        n, j = p * NR + step, step % 2
                        pe.wait_ge(q_ready, n * 2 + 2)
                        pe.wait_ge(biased, n + 1)
                        nc.tensor.matmul(s_ps[j][:, 0:nk], qb[j][:, :], qk[:, bass.ds(p + CT, 1), k0:k0 + nk],
                                         start=True, stop=True).then_inc(scores, 1)
                    if 2 <= step <= NR + 1:
                        r = step - 2
                        nk, n, j, b = ROWS[r][2], p * NR + r, r % 2, r % NB
                        pe.wait_ge(normed, n + 1)
                        pe.wait_ge(turned_c, n + 1)
                        for m in range(nk // P):
                            last = nc.tensor.transpose(t_ps[j][:, m * P:(m + 1) * P],
                                                       pr[b][:, m * P:(m + 1) * P], ident)
                        last.then_inc(turned, 1)
                    if step >= 3:
                        r = step - 3
                        (q0, k0, nk, dr), n, j = ROWS[r], p * NR + r, r % 2
                        if r == 0:
                            pe.wait_ge(v_in, p * 32 + 32)
                        pe.wait_ge(turned_c, n + 3)
                        pe.wait_ge(o_ready, n + 1)
                        for m in range(nk // P):
                            at = k0 + m * P
                            v = v_even[:, at // P, :] if at % P == 0 else v_odd[:, (at - GRID_W) // P, :]
                            last = nc.tensor.matmul(o_ps[j][:, 0:P], v, prT[j][:, m * P:(m + 1) * P],
                                                    start=m == 0, stop=m == nk // P - 1)
                        last.then_inc(pv_done, 1)

        @block.scalar
        def _(act):
            act.sem_inc(exped, NB)
            act.sem_inc(turned_c, 2)
            with nc.allow_non_contiguous_dma(reason="bias rows, one shifted row for a query column"):
                for h in range(2 * CT):
                    rows = slice(h % 2 * GRID_W, (h % 2 + 1) * GRID_W)
                    width = 2 * GRID_W - 1
                    src = rpb[h, :, 0:GRID_W]
                    src = bass.AP(tensor=src.tensor, offset=src.offset,
                                  ap=[[1, GRID_W], [width, NDR], [1, GRID_W]])
                    act.dma_start(bias[rows, h // 2, :].rearrange("p (r c) -> p r c", c=GRID_W), src
                                  ).then_inc(bias_in, 16)
                act.dma_start(cms[:, :], cm).then_inc(bias_in, 16)
            with act.Fori(0, CT) as p:
                for step in range(NR + 2):
                    if step < NR:
                        nk, n, b = ROWS[step][2], p * NR + step, step % NB
                        act.wait_ge(shift_ready, n + 1)
                        act.wait_ge(turned, n + 1)
                        nc.scalar.activation(pr[b][:, 0:nk], sc[b][:, 0:nk], ACT.Exp, bias=st[b][:, 1:2],
                                             accum_out=st[b][:, 2:3]).then_inc(exped, 1)
                    if step >= 2:
                        r = step - 2
                        nk, n, j = ROWS[r][2], p * NR + r, r % 2
                        act.wait_ge(turned, n + (1 + NB))
                        act.wait_ge(pv_done, n + 1)
                        nc.scalar.activation(prT[j][:, 0:nk], t_ps[j][:, 0:nk], ACT.Copy
                                             ).then_inc(turned_c, 1)

        @block.vector
        def _(dve):
            dve.sem_inc(biased, 2)
            dve.sem_inc(o_ready, 2)
            dve.wait_ge(bias_in, 16 * 9)
            flat = bias[:, :, :].rearrange("p n (r c) -> p (n r) c", c=GRID_W)
            nc.vector.tensor_tensor(flat, flat, cms[:, :].unsqueeze(1).to_broadcast([P, CT * NDR, GRID_W]),
                                    ALU.add).then_inc(bias_ready, 1)
            dve.wait_ge(bias_ready, 1)
            with dve.Fori(0, CT) as p:
                for step in range(NR + 3):
                    if step < NR:
                        q0, k0, nk, dr = ROWS[step]
                        n, j, b = p * NR + step, step % 2, step % NB
                        dve.wait_ge(scores, n + 3)
                        dve.wait_ge(exped, n + 1)
                        nc.vector.scalar_tensor_tensor(
                            sc[b][:, 0:nk], s_ps[j][:, 0:nk], HD ** -0.5,
                            bias[:, bass.ds(p, 1), dr * GRID_W:dr * GRID_W + nk],
                            ALU.mult, ALU.add).then_inc(biased, 1)
                    if 1 <= step <= NR:
                        r = step - 1
                        nk, n, b = ROWS[r][2], p * NR + r, r % NB
                        dve.wait_ge(exped, n + (1 + NB))
                        nc.vector.reciprocal(st[b][:, 3:4], st[b][:, 2:3]).then_inc(summed, 1)
                    if step < NR:
                        nk, n, b = ROWS[step][2], p * NR + step, step % NB
                        dve.wait_ge(biased, n + 3)
                        nc.vector.tensor_reduce(st[b][:, 1:2], sc[b][:, 0:nk], AX.X, ALU.max, negate=True
                                                ).then_inc(shift_ready, 1)
                    if 1 <= step <= NR:
                        r = step - 1
                        nk, n, b = ROWS[r][2], p * NR + r, r % NB
                        dve.wait_ge(summed, n + 1)
                        nc.vector.tensor_scalar(pr[b][:, 0:nk], pr[b][:, 0:nk], st[b][:, 3:4], None,
                                                ALU.mult).then_inc(normed, 1)
                    if step >= 3:
                        r = step - 3
                        q0, n, j = ROWS[r][0], p * NR + r, r % 2
                        dve.wait_ge(pv_done, n + 3)
                        for h in range(2):
                            rows = slice(h * HD, (h + 1) * HD)
                            last = nc.vector.tensor_scalar(oT[rows, bass.ds(p, 1), q0:q0 + GRID_W],
                                                           o_ps[j][rows, backwards(h)], 1.0, None,
                                                           ALU.mult)
                        last.then_inc(o_ready, 1)
            dve.wait_ge(o_ready, CT * NR + 2)


def gate_projection(nc, w_in, params, H, g_dram):
    E_G = 2 * KD
    with ExitStack() as ctx:
        zero = params[:, PM_ZERO:PM_ZERO + 1]
        sb = lambda n, s: ctx.enter_context(nc.sbuf_tensor(n, s, F32))
        sem = lambda n: ctx.enter_context(nc.semaphore("gp_" + n))
        w = [sb(f"gp_w{j}", [P, D]) for j in range(2)]
        wp = [split_tiles(ctx, nc, f"gp_wp{j}", [P, D]) for j in range(2)]
        gb = [sb(f"gp_g{j}", [P, T]) for j in range(2)]
        ps = [ctx.enter_context(nc.psum_tensor(f"gp_ps{j}", [P, 1536], F32)) for j in range(2)]
        w_ld = [sem(f"w_ld{j}") for j in range(2)]
        g_out = [sem(f"g_out{j}") for j in range(2)]
        gemm, g_ready, high_done, split, stored = (
            sem("gemm"), sem("g"), sem("high"), sem("split"), sem("stored"))
        block = ctx.enter_context(nc.Block())

        @block.sync
        def _(sp):
            with sp.Fori(0, E_G // 2) as i:
                for j in range(2):
                    e = i * 2 + j
                    sp.wait_ge(split, e + 1)
                    sp.dma_start(w[j][:, :], w_in[e + E_G0, :, :]).then_inc(w_ld[j], 16)

        @block.gpsimd
        def _(pool):
            pool.sem_inc(split, 2)
            with pool.Fori(0, E_G // 2) as i:
                for j in range(2):
                    e = i * 2 + j
                    pool.wait_ge(gemm, e * NG + NG)
                    split_weights(pool, nc, zero, w[j][:, :], wp[j], w_ld[j], high_done, split, i, e)

        @block.tensor
        def _(pe):
            pe.sem_inc(gemm, 2 * NG)
            with pe.Fori(0, E_G // 2) as i:
                for j in range(2):
                    e = i * 2 + j
                    pe.wait_ge(split, e + 3)
                    for g, (t0, tn) in enumerate(GROUPS):
                        pe.wait_ge(g_ready, e * NG + (g + 1))
                        for k in range(KD):
                            last = products(nc, ps[j][:, t0:t0 + tn], [a[:, k * P:(k + 1) * P] for a in wp[j]],
                                            [h[:, k, t0:t0 + tn] for h in H], k == 0, k == KD - 1)
                        last.then_inc(gemm, 1)

        @block.scalar
        def _(act):
            act.sem_inc(stored, 2)
            with act.Fori(0, E_G // 2) as i:
                for j in range(2):
                    e = i * 2 + j
                    act.wait_ge(g_ready, e * NG + 3 * NG)
                    act.dma_start(g_dram[e, :, :], gb[j][:, :]).then_inc(g_out[j], 16)
                    act.wait_ge(g_out[j], i * 16 + 16)
                    act.sem_inc(stored, 1)

        @block.vector
        def _(dve):
            dve.sem_inc(g_ready, 2 * NG)
            with dve.Fori(0, E_G // 2) as i:
                for j in range(2):
                    e = i * 2 + j
                    dve.wait_ge(stored, e + 1)
                    for g, (t0, tn) in enumerate(GROUPS):
                        dve.wait_ge(gemm, e * NG + (2 * NG + g + 1))
                        nc.vector.tensor_scalar(gb[j][:, t0:t0 + tn], ps[j][:, t0:t0 + tn],
                                                params[:, bass.ds(e + PM_BG, 1)], None, ALU.add
                                                ).then_inc(g_ready, 1)


def merge_branches(nc, w_proj, g_dram, oa_dram, obT, m_dram):
    with ExitStack() as ctx:
        sb = lambda n, s: ctx.enter_context(nc.sbuf_tensor(n, s, F32))
        sem = lambda n: ctx.enter_context(nc.semaphore("mb_" + n))
        oaT = sb("mb_oa", [P, CT, T])
        w = [sb(f"mb_w{j}", [P, D]) for j in range(2)]
        gate = [sb(f"mb_gate{j}", [P, 2, T]) for j in range(2)]
        mo = [sb(f"mb_mo{j}", [P, T]) for j in range(2)]
        ps = [ctx.enter_context(nc.psum_tensor(f"mb_ps{j}", [P, 2, 512], F32)) for j in range(4)]
        oa_in, gated, proj, gemm, parts, merged, stored = (
            sem("oa_in"), sem("gated"), sem("proj"), sem("gemm"), sem("parts"), sem("merged"),
            sem("stored"))
        w_ld = [sem(f"w_ld{j}") for j in range(2)]
        g_ld = [sem(f"g_ld{j}") for j in range(2)]
        m_out = [sem(f"m_out{j}") for j in range(2)]
        gr = g_dram.rearrange("(h c) p t -> c p h t", h=2)
        block = ctx.enter_context(nc.Block())

        @block.sync
        def _(sp):
            sp.dma_start(oaT[:, :, :], oa_dram).then_inc(oa_in, 16)
            with sp.Fori(0, KD // 2) as i:
                for j in range(2):
                    c = i * 2 + j
                    sp.wait_ge(merged, c * NG + NG)
                    sp.dma_start(w[j][:, :], w_proj[c, :, :]).then_inc(w_ld[j], 16)
                    sp.dma_start(gate[j][:, :, :], gr[c, :, :, :]).then_inc(g_ld[j], 16)

        @block.gpsimd
        def _(pool):
            pool.sem_inc(stored, 2)
            with pool.Fori(0, KD // 2) as i:
                for j in range(2):
                    c = i * 2 + j
                    pool.wait_ge(merged, c * NG + 3 * NG)
                    pool.dma_start(m_dram[c, :, :], mo[j][:, :]).then_inc(m_out[j], 16)
                    pool.wait_ge(m_out[j], i * 16 + 16)
                    pool.sem_inc(stored, 1)

        @block.tensor
        def _(pe):
            pe.wait_ge(oa_in, 16)
            with pe.Fori(0, KD // 2) as i:
                for j in range(2):
                    pe.wait_ge(w_ld[j], i * 16 + 16)
                    for g, (t0, tn) in enumerate(GROUPS):
                        u, b = (i * 2 + j) * NG + g, (j * NG + g) % 2
                        pe.wait_ge(parts, u + 1)
                        for out, src in enumerate((oaT, obT)):
                            for k in range(CT):
                                at = (out * CT + k) * P
                                last = nc.tensor.matmul(ps[b][:, out, 0:tn], w[j][:, at:at + P],
                                                        src[:, k, t0:t0 + tn],
                                                        start=k == 0, stop=k == CT - 1)
                        last.then_inc(gemm, 1)

        @block.scalar
        def _(act):
            with act.Fori(0, KD // 2) as i:
                for j in range(2):
                    act.wait_ge(g_ld[j], i * 16 + 16)
                    nc.scalar.activation(gate[j][:, :, :], gate[j][:, :, :], ACT.Sigmoid).then_inc(gated, 1)

        @block.vector
        def _(dve):
            dve.sem_inc(parts, 2)
            dve.sem_inc(merged, 2 * NG)
            with dve.Fori(0, KD // 2) as i:
                for j in range(2):
                    c = i * 2 + j
                    dve.wait_ge(gated, c + 1)
                    dve.wait_ge(stored, c + 1)
                    for g, (t0, tn) in enumerate(GROUPS):
                        u, b = c * NG + g, (j * NG + g) % 2
                        both = gate[j][:, :, t0:t0 + tn]
                        dve.wait_ge(gemm, u + 1)
                        nc.vector.tensor_tensor(both, both, ps[b][:, :, 0:tn], ALU.mult).then_inc(parts, 1)
                        dve.wait_ge(parts, u + 3)
                        nc.vector.tensor_tensor(mo[j][:, t0:t0 + tn], gate[j][:, 0, t0:t0 + tn],
                                                gate[j][:, 1, t0:t0 + tn], ALU.add).then_inc(merged, 1)


def output_projection(nc, x, w_out, gains, params, ident, m_dram, x1_dram, H):
    with ExitStack() as ctx:
        zero = params[:, PM_ZERO:PM_ZERO + 1]
        sb = lambda n, s: ctx.enter_context(nc.sbuf_tensor(n, s, F32))
        sem = lambda n: ctx.enter_context(nc.semaphore("op_" + n))
        xs = [sb(f"op_x{j}", [P, D]) for j in range(2)]
        ms = [sb(f"op_m{j}", [P, KD, P]) for j in range(2)]
        mp = [split_tiles(ctx, nc, f"op_mp{j}", [P, KD, P]) for j in range(2)]
        wr = [sb(f"op_wr{j}", [P, D]) for j in range(2)]
        wo = split_tiles(ctx, nc, "op_wo", [P, KD, D])
        hb = wr[1][:, :].rearrange("p (k t) -> p k t", k=KD)
        sq = wr[0]
        yb = [sb(f"op_y{j}", [P, D]) for j in range(2)]
        gain = sb("op_gain", [P, D])
        xo = [sb(f"op_xo{j}", [P, D]) for j in range(2)]
        st = [sb(f"op_st{j}", [P, 6]) for j in range(2)]
        pg = [ctx.enter_context(nc.psum_tensor(f"op_pg{j}", [P, D], F32)) for j in range(2)]
        pt = [ctx.enter_context(nc.psum_tensor(f"op_pt{j}", [P, D], F32)) for j in range(2)]
        x_in = [sem(f"x_in{j}") for j in range(2)]
        x_out = [sem(f"x_out{j}") for j in range(2)]
        stored, high, low, w_high, w_split, m_high = (
            sem("stored"), sem("high"), sem("low"), sem("w_high"), sem("w_split"), sem("m_high"))
        w_high_v, w_split_v = sem("w_high_v"), sem("w_split_v")
        stage = wr + yb + xo
        NST = len(stage)
        BY_POOL = [0, 3, 6]
        BY_DVE = [k for k in range(KD) if k not in BY_POOL]
        w_ld = [sem(f"w_ld{j}") for j in range(NST)]
        m_ld = [sem(f"m_ld{j}") for j in range(2)]
        mr = m_dram.rearrange("k p t -> p k t")
        g_in, staged, gemm, sq1, rms1, inv1, scaled, x1_ready = (
            sem("g_in"), sem("staged"), sem("gemm"), sem("sq1"), sem("rms1"),
            sem("inv1"), sem("scaled"), sem("x1"))
        sq2, rms2, inv2, xn_ready, turned, h_ready = (
            sem("sq2"), sem("rms2"), sem("inv2"), sem("xn"), sem("turned"), sem("h"))
        xr = x.rearrange("(n p) d -> n p d", p=P)
        x1r = x1_dram.rearrange("(n p) d -> n p d", p=P)
        block = ctx.enter_context(nc.Block())

        @block.sync
        def _(sp):
            for k in range(KD):
                if k >= NST:
                    last = k - NST
                    mine, split_ = (BY_POOL, w_split) if last in BY_POOL else (BY_DVE, w_split_v)
                    sp.wait_ge(split_, mine.index(last) + 1)
                sp.dma_start(stage[k % NST][:, :], w_out[:, k, :]).then_inc(w_ld[k % NST], 16)
            sp.dma_start(gain[:, :], gains[0, :].partition_broadcast(P)).then_inc(g_in, 16)
            with sp.Fori(0, NT // 2) as i:
                for j in range(2):
                    n = i * 2 + j
                    sp.wait_ge(staged, n + 1)
                    sp.dma_start(ms[j][:, :, :], mr[:, :, bass.ts(n, P)]).then_inc(m_ld[j], 16)
                    sp.wait_ge(x1_ready, n + 1)
                    sp.dma_start(xs[j][:, :], xr[n, :, :]).then_inc(x_in[j], 16)

        @block.gpsimd
        def _(pool):
            pool.sem_inc(stored, 2)
            pool.sem_inc(staged, 2)
            for n, k in enumerate(BY_POOL):
                split_weights(pool, nc, zero, stage[k % NST][:, :], [a[:, k, :] for a in wo],
                              w_ld[k % NST], w_high, w_split, k // NST, n)

            def split(n, j, i):
                pool.wait_ge(gemm, n + 1)
                split_weights(pool, nc, zero, ms[j][:, :, :], mp[j], m_ld[j], m_high, staged, i, n)

            def store(n, j, i):
                pool.wait_ge(x1_ready, n + 3)
                pool.dma_start(x1r[bass.ds(n, 1), :, :].rearrange("o p d -> (o p) d"), xo[j][:, :]
                               ).then_inc(x_out[j], 16)
                pool.wait_ge(x_out[j], i * 16 + 16)
                pool.sem_inc(stored, 1)

            split(0, 0, 0)
            split(1, 1, 0)
            with pool.Fori(0, NT // 2 - 1) as i:
                for j in range(2):
                    split(i * 2 + (j + 2), j, i + 1)
                    store(i * 2 + j, j, i)
            store(NT - 2, 0, NT // 2 - 1)
            store(NT - 1, 1, NT // 2 - 1)

        @block.tensor
        def _(pe):
            pe.sem_inc(gemm, 2)
            pe.sem_inc(turned, 2)
            pe.wait_ge(w_split, len(BY_POOL))
            pe.wait_ge(w_split_v, len(BY_DVE))

            def project(n, j):
                pe.wait_ge(staged, n + 3)
                pe.wait_ge(scaled, n + 1)
                for h in range(2):
                    for k in range(KD):
                        last = products(nc, pg[j][:, h * 512:(h + 1) * 512], [a[:, k, :] for a in mp[j]],
                                        [a[:, k, h * 512:(h + 1) * 512] for a in wo],
                                        k == 0, k == KD - 1)
                last.then_inc(gemm, 1)

            def turn(n, j):
                pe.wait_ge(xn_ready, n + 3)
                pe.wait_ge(h_ready, n + 1)
                for k in range(KD):
                    last = nc.tensor.transpose(pt[j][:, k * P:(k + 1) * P],
                                               yb[j][:, k * P:(k + 1) * P], ident)
                last.then_inc(turned, 1)

            project(0, 0)
            with pe.Fori(0, NT // 2 - 1) as i:
                for j in range(2):
                    project(i * 2 + (j + 1), 1 - j)
                    turn(i * 2 + j, j)
            project(NT - 1, 1)
            turn(NT - 2, 0)
            turn(NT - 1, 1)

        @block.scalar
        def _(act):
            with act.Fori(0, NT // 2) as i:
                for j in range(2):
                    n = i * 2 + j
                    s = st[j]
                    act.wait_ge(gemm, n + 3)
                    nc.scalar.activation(sq[:, :], pg[j][:, :], ACT.Square, accum_out=s[:, 0:1]
                                         ).then_inc(sq1, 1)
                    act.wait_ge(sq1, n + 1)
                    nc.scalar.activation(s[:, 1:2], s[:, 0:1], ACT.Sqrt, scale=1.0 / D,
                                         bias=params[:, PM_EPS:PM_EPS + 1]).then_inc(rms1, 1)
                    act.wait_ge(x1_ready, n + 3)
                    nc.scalar.activation(sq[:, :], xo[j][:, :], ACT.Square, accum_out=s[:, 3:4]
                                         ).then_inc(sq2, 1)
                    act.wait_ge(sq2, n + 1)
                    nc.scalar.activation(s[:, 4:5], s[:, 3:4], ACT.Sqrt, scale=1.0 / D,
                                         bias=params[:, PM_EPS:PM_EPS + 1]).then_inc(rms2, 1)

        @block.vector
        def _(dve):
            for s in (scaled, x1_ready, xn_ready, h_ready):
                dve.sem_inc(s, 2)
            for n, k in enumerate(BY_DVE):
                raw = stage[k % NST][:, :]
                dve.wait_ge(w_ld[k % NST], (k // NST + 1) * 16)
                nc.vector.tensor_copy(wo[0][:, k, :], raw).then_inc(w_high_v, 1)
                dve.wait_ge(w_high_v, n + 1)
                nc.vector.tensor_tensor(wo[1][:, k, :], raw, wo[0][:, k, :].bitcast(F32),
                                        ALU.subtract).then_inc(w_split_v, 1)
            dve.wait_ge(g_in, 16)

            def finish(n, j):
                dve.wait_ge(turned, n + 3)
                nc.vector.tensor_tensor(
                    hb[:, :, :], pt[j][:, :].rearrange("p (k t) -> p k t", k=KD),
                    params[:, PM_G2:PM_G2 + KD].unsqueeze(2).to_broadcast([P, KD, P]),
                    ALU.mult).then_inc(h_ready, 1)
                dve.wait_ge(h_ready, n + 3)
                nc.vector.tensor_copy(H[0][:, :, bass.ts(n, P)], hb[:, :, :]).then_inc(high, 1)
                dve.wait_ge(high, n + 1)
                nc.vector.tensor_tensor(H[1][:, :, bass.ts(n, P)], hb[:, :, :],
                                        H[0][:, :, bass.ts(n, P)].bitcast(F32),
                                        ALU.subtract).then_inc(low, 1)
                dve.wait_ge(low, n + 1)

            with dve.Fori(0, NT // 2) as i:
                for j in range(2):
                    n = i * 2 + j
                    s = st[j]
                    dve.wait_ge(rms1, n + 1)
                    nc.vector.reciprocal(s[:, 2:3], s[:, 1:2]).then_inc(inv1, 1)
                    dve.wait_ge(inv1, n + 1)
                    dve.wait_ge(turned, n + 1)
                    nc.vector.scalar_tensor_tensor(yb[j][:, :], pg[j][:, :], s[:, 2:3], gain[:, :],
                                                   ALU.mult, ALU.mult).then_inc(scaled, 1)
                    dve.wait_ge(scaled, n + 3)
                    dve.wait_ge(x_in[j], i * 16 + 16)
                    dve.wait_ge(stored, n + 1)
                    nc.vector.tensor_tensor(xo[j][:, :], yb[j][:, :], xs[j][:, :], ALU.add
                                            ).then_inc(x1_ready, 1)
                    dve.wait_ge(rms2, n + 1)
                    nc.vector.reciprocal(s[:, 5:6], s[:, 4:5]).then_inc(inv2, 1)
                    dve.wait_ge(inv2, n + 1)
                    nc.vector.tensor_scalar(yb[j][:, :], xo[j][:, :], s[:, 5:6], None, ALU.mult
                                            ).then_inc(xn_ready, 1)
                    finish(n, j)
            dve.wait_ge(h_ready, NT + 2)


def feed_forward(nc, params, w_up, w_down, H, f):
    with ExitStack() as ctx:
        zero = params[:, PM_ZERO:PM_ZERO + 1]
        sb = lambda n, s: ctx.enter_context(nc.sbuf_tensor(n, s, F32))
        sem = lambda n: ctx.enter_context(nc.semaphore("ff_" + n))
        wr = [sb(f"ff_wr{j}", [P, D]) for j in range(2)]
        wu = [split_tiles(ctx, nc, f"ff_wu{j}", [P, D]) for j in range(FT)]
        wd = [split_tiles(ctx, nc, f"ff_wd{j}", [P, D]) for j in range(FT)]
        G = split_tiles(ctx, nc, "ff_g", [P, FT, T])
        rl = [sb(f"ff_rl{j}", [P, 512]) for j in range(2)]
        sq = [sb(f"ff_sq{j}", [P, 512]) for j in range(2)]
        pu = [ctx.enter_context(nc.psum_tensor(f"ff_pu{j}", [P, 512], F32)) for j in range(3)]
        pd = [ctx.enter_context(nc.psum_tensor(f"ff_pd{j}", [P, 512], F32)) for j in range(4)]
        w_ld = [sem(f"w_ld{j}") for j in range(2)]
        high_done, split, up, relu, squared, g_high, g_ready, zeroed, down, added = (
            sem("high"), sem("split"), sem("up"), sem("relu"), sem("squared"), sem("g_high"),
            sem("g"), sem("zeroed"), sem("down"), sem("added"))
        NU, ND = FT * NG, NT * 2
        NW = 2 * FT
        block = ctx.enter_context(nc.Block())

        @block.sync
        def _(sp):
            with sp.Fori(0, FG) as g:
                for m in range(NW):
                    sp.wait_ge(split, g * NW + (m + 1))
                    src = w_up[g * FT + m, :, :] if m < FT else w_down[g * FT + (m - FT), :, :]
                    sp.dma_start(wr[m % 2][:, :], src).then_inc(w_ld[m % 2], 16)

        @block.gpsimd
        def _(pool):
            pool.sem_inc(split, 2)
            with pool.Fori(0, FG) as g:
                for m in range(NW):
                    if m < FT:
                        pool.wait_ge(up, g * NU + (m + 1) * NG)
                    else:
                        pool.wait_ge(down, g * ND + 1)
                    pool.wait_ge(w_ld[m % 2], g * (NW // 2 * 16) + (m // 2 + 1) * 16)
                    to = wu[m] if m < FT else wd[m - FT]
                    nc.gpsimd.tensor_tensor(to[0], wr[m % 2][:, :], zero_like(wr[m % 2][:, :], zero),
                                            ALU.add).then_inc(high_done, 1)
                    pool.wait_ge(high_done, g * NW + (m + 1))
                    nc.gpsimd.tensor_tensor(to[1], wr[m % 2][:, :], to[0].bitcast(F32), ALU.subtract
                                            ).then_inc(split, 1)

        @block.tensor
        def _(pe):
            pe.sem_inc(up, NU)
            pe.sem_inc(down, 1)
            with pe.Fori(0, FG) as g:
                for m in range(FT):
                    pe.wait_ge(split, g * NW + (m + 3))
                    for b, (t0, tn) in enumerate(GROUPS):
                        pe.wait_ge(relu, g * NU + (m * NG + b + 1))
                        for k in range(KD):
                            last = products(nc, pu[b][:, 0:tn], [a[:, k * P:(k + 1) * P] for a in wu[m]],
                                            [h[:, k, t0:t0 + tn] for h in H], k == 0, k == KD - 1)
                        last.then_inc(up, 1)
                pe.wait_ge(split, g * NW + (NW + 2))
                for n in range(NT):
                    b = next(b for b, (t0, tn) in enumerate(GROUPS) if n * P < t0 + tn)
                    pe.wait_ge(g_ready, g * NU + ((FT - 1) * NG + b + 1))
                    for h in range(2):
                        d = 2 * n + h
                        pe.wait_ge(added, g * ND + (d + 1))
                        for m in range(FT):
                            last = products(nc, pd[d % 4][:, :], [a[:, m, n * P:(n + 1) * P] for a in G],
                                            [a[:, h * 512:(h + 1) * 512] for a in wd[m]],
                                            m == 0, m == FT - 1)
                        last.then_inc(down, 1)

        @block.scalar
        def _(act):
            act.sem_inc(relu, 3)
            with act.Fori(0, FG) as g:
                for u in range(NU + 1):
                    if u < NU:
                        b, tn = u % NG, GROUPS[u % NG][1]
                        act.wait_ge(up, g * NU + (NU + u + 1))
                        act.wait_ge(squared, g * NU + (u + 1))
                        nc.scalar.activation(rl[u % 2][:, 0:tn], pu[b][:, 0:tn], ACT.Relu
                                             ).then_inc(relu, 1)
                    if u >= 1:
                        v = u - 1
                        m, (t0, tn) = v // NG, GROUPS[v % NG]
                        act.wait_ge(squared, g * NU + (v + 3))
                        if v < NG:
                            act.wait_ge(down, g * ND + 1)
                        nc.scalar.activation(G[0][:, m, t0:t0 + tn], sq[v % 2][:, 0:tn], ACT.Copy
                                             ).then_inc(g_high, 1)

        @block.vector
        def _(dve):
            dve.sem_inc(added, 4)
            dve.sem_inc(squared, 2)
            nc.vector.memset(f, 0.0).then_inc(zeroed, 1)
            dve.wait_ge(zeroed, 1)
            with dve.Fori(0, FG) as g:
                for u in range(NU + 1):
                    if u < NU:
                        tn = GROUPS[u % NG][1]
                        dve.wait_ge(relu, g * NU + (u + 4))
                        if u >= 2:
                            dve.wait_ge(g_ready, g * NU + (u - 1))
                        nc.vector.tensor_tensor(sq[u % 2][:, 0:tn], rl[u % 2][:, 0:tn],
                                                rl[u % 2][:, 0:tn], ALU.mult).then_inc(squared, 1)
                    if u >= 1:
                        v = u - 1
                        m, (t0, tn) = v // NG, GROUPS[v % NG]
                        dve.wait_ge(g_high, g * NU + (v + 1))
                        nc.vector.tensor_tensor(G[1][:, m, t0:t0 + tn], sq[v % 2][:, 0:tn],
                                                G[0][:, m, t0:t0 + tn].bitcast(F32), ALU.subtract
                                                ).then_inc(g_ready, 1)
                for d in range(ND):
                    n, h = d // 2, d % 2
                    dve.wait_ge(down, g * ND + (d + 2))
                    at = f[:, n, h * 512:(h + 1) * 512]
                    nc.vector.tensor_tensor(at, at, pd[d % 4][:, :], ALU.add).then_inc(added, 1)
            dve.wait_ge(added, FG * ND + 4)


def final_norm(nc, gains, params, f, x1_dram, out):
    NBUF = 5
    assert NT % NBUF == 0
    with ExitStack() as ctx:
        sb = lambda n, s: ctx.enter_context(nc.sbuf_tensor(n, s, F32))
        sem = lambda n: ctx.enter_context(nc.semaphore("fn_" + n))
        gain, sq = sb("fn_gain", [P, D]), sb("fn_sq", [P, D])
        xs = [sb(f"fn_x{j}", [P, D]) for j in range(NBUF)]
        ob = [sb(f"fn_o{j}", [P, D]) for j in range(NBUF)]
        st = [sb(f"fn_st{j}", [P, 3]) for j in range(NBUF)]
        x_in = [sem(f"x_in{j}") for j in range(NBUF)]
        o_out = [sem(f"o_out{j}") for j in range(NBUF)]
        stored = sem("stored")
        g_in, squared, rms, inv, scaled, o_ready = (
            sem("g_in"), sem("sq"), sem("rms"), sem("inv"), sem("scaled"), sem("o"))
        x1r = x1_dram.rearrange("(n p) d -> n p d", p=P)
        outr = out.rearrange("(n p) d -> n p d", p=P)
        block = ctx.enter_context(nc.Block())

        @block.sync
        def _(sp):
            sp.dma_start(gain[:, :], gains[1, :].partition_broadcast(P)).then_inc(g_in, 16)
            with sp.Fori(0, NT // NBUF) as i:
                for j in range(NBUF):
                    n = i * NBUF + j
                    sp.wait_ge(o_ready, n + 1)
                    sp.dma_start(xs[j][:, :], x1r[n, :, :]).then_inc(x_in[j], 16)

        @block.gpsimd
        def _(pool):
            pool.sem_inc(stored, NBUF)
            with pool.Fori(0, NT // NBUF) as i:
                for j in range(NBUF):
                    n = i * NBUF + j
                    pool.wait_ge(o_ready, n + (1 + NBUF))
                    pool.dma_start(outr[n, :, :], ob[j][:, :]).then_inc(o_out[j], 16)
                    pool.wait_ge(o_out[j], i * 16 + 16)
                    pool.sem_inc(stored, 1)

        @block.scalar
        def _(act):
            with act.Fori(0, NT // NBUF) as i:
                for j in range(NBUF):
                    n = i * NBUF + j
                    act.wait_ge(scaled, n + 1)
                    nc.scalar.activation(sq[:, :], f[:, bass.ds(n, 1), :], ACT.Square,
                                         accum_out=st[j][:, 0:1]).then_inc(squared, 1)
                    act.wait_ge(squared, n + 1)
                    nc.scalar.activation(st[j][:, 1:2], st[j][:, 0:1], ACT.Sqrt, scale=1.0 / D,
                                         bias=params[:, PM_EPS:PM_EPS + 1]).then_inc(rms, 1)

        @block.vector
        def _(dve):
            dve.sem_inc(o_ready, NBUF)
            dve.sem_inc(scaled, NBUF)
            dve.wait_ge(g_in, 16)
            with dve.Fori(0, NT // NBUF) as i:
                for j in range(NBUF):
                    n = i * NBUF + j
                    dve.wait_ge(rms, n + 1)
                    nc.vector.reciprocal(st[j][:, 2:3], st[j][:, 1:2]).then_inc(inv, 1)
                    dve.wait_ge(inv, n + 1)
                    dve.wait_ge(stored, n + 1)
                    nc.vector.scalar_tensor_tensor(ob[j][:, :], f[:, bass.ds(n, 1), :], st[j][:, 2:3],
                                                   gain[:, :], ALU.mult, ALU.mult).then_inc(scaled, 1)
                    dve.wait_ge(scaled, n + (1 + NBUF))
                    dve.wait_ge(x_in[j], i * 16 + 16)
                    nc.vector.tensor_tensor(ob[j][:, :], ob[j][:, :], xs[j][:, :], ALU.add
                                            ).then_inc(o_ready, 1)


def encoder(nc, a, out):
    dram = lambda n, s: nc.dram_tensor(n, s, F32).ap()
    v_dram, oa_dram, x1_dram = dram("v_dram", [T, 512]), dram("oa_dram", [P, CT, T]), dram("x1_dram", [T, D])
    g_dram, m_dram = dram("g_dram", [2 * KD, P, T]), dram("m_dram", [KD, P, T])
    with ExitStack() as ctx:
        sb = lambda n, s: ctx.enter_context(nc.sbuf_tensor(n, s, F32))
        params, cn = sb("params", [P, PM_N]), sb("cn", [P, CN_N])
        ident, ones, mean = (cn[:, c:c + P] for c in (CN_ID, CN_ONES, CN_MEAN))
        with nc.semaphore("const_in") as const_in, nc.Block() as block:
            @block.sync
            def _(sp):
                sp.dma_start(params[:, :], a["params"]).then_inc(const_in, 16)
                sp.dma_start(cn[:, :], a["cn"]).then_inc(const_in, 16)
                sp.wait_ge(const_in, 32)
        with nc.sbuf_tensor("sT", [P, E_SH, T], F32) as sT:
            with ExitStack() as up:
                H = split_tiles(up, nc, "h1", [P, KD, T])
                norm_to_channels(nc, a["x"], params, ident, H)
                qk = sT[:, 0:2 * CT, :]
                attention_projection(nc, params, a["w_in"], a["w_v"], v_dram, H, qk)
                attention(nc, a["rpb"], a["cm"], v_dram, oa_dram, ident, qk, sT[:, 0:CT, :])
                shifted_projection(nc, a["w_in"], params, H, sT)
                gate_projection(nc, a["w_in"], params, H, g_dram)
            with nc.sbuf_tensor("ab", [P, 16 * T], F32) as ab:
                scan_mixer(nc, a["lora"], params, a["cs"], ident, ones, mean, ab, sT)
            merge_branches(nc, a["w_proj"], g_dram, oa_dram, sT[:, 0:CT, :], m_dram)
        with ExitStack() as up:
            H = split_tiles(up, nc, "h2", [P, KD, T])
            output_projection(nc, a["x"], a["w_out"], a["gains"], params, ident, m_dram, x1_dram, H)
            f = up.enter_context(nc.sbuf_tensor("f", [P, NT, D], F32))[:, :, :]
            feed_forward(nc, params, a["w_up"], a["w_down"], H, f)
            final_norm(nc, a["gains"], params, f, x1_dram, out)



def host_constants():
    import numpy as np
    eye = np.eye(P, dtype=np.float32)
    heads = np.kron(np.eye(2, dtype=np.float32), np.ones((HD, HD), np.float32))
    cn = np.concatenate([eye, heads, heads / HD], axis=1)
    reset = np.ones(T, np.float32)
    reset[::C] = 0
    keep = np.ones((2, NC), np.float32)
    keep[0, [NC_P - 1, NC - 1]] = 0
    keep[1, [0, NC_P]] = 0
    i = np.arange(P)
    s, t = i[:, None], i[None, :]
    same = (s // C) == (t // C)
    parts = [np.broadcast_to(reset, (P, T)), np.broadcast_to(keep.reshape(-1), (P, 2 * NC))]
    before = [s < t, s > t]
    for d in range(2):
        strict, incl = same & before[d], same & (before[d] | (s == t))
        parts += [strict, incl] if d == 0 else [incl, strict]
    joins = lambda d, b: (s // b == t // b) & (s // (b // 2) != t // (b // 2)) & before[d]
    for d in range(2):
        parts.append(joins(d, 2))
    for d in range(2):
        parts += [joins(d, 4 << l) for l in range(LEVELS)]
    cs = np.concatenate([np.asarray(p, np.float32) for p in parts], axis=1)
    c = np.arange(GRID_W)
    start = np.clip(c - WIN_W // 2, 0, GRID_W - WIN_W)
    ok = (c[None, :] >= start[:, None]) & (c[None, :] < start[:, None] + WIN_W)
    cm = np.tile(np.where(ok, 0.0, NEG).astype(np.float32)[::-1], (2, 1))
    return cn.astype(np.float32), np.ascontiguousarray(cs), np.ascontiguousarray(cm)


def host_layout(a):
    import numpy as np
    col = lambda v: np.asarray(v).reshape(-1, P).T
    slabs = lambda w: np.ascontiguousarray(
        w.reshape(w.shape[0] // P, P, w.shape[1] // P, P).transpose(2, 1, 0, 3)
        .reshape(w.shape[1] // P, P, w.shape[0]))
    rows = lambda w: np.ascontiguousarray(
        w.reshape(w.shape[0] // P, P, w.shape[1]).transpose(1, 0, 2))
    w_in = a["w_in"][0]
    per_pair = np.stack([col(a["w0"][0][0]), col(a["w0"][0][1]), col(a["a0"][0][0]), col(a["a0"][0][1]),
                         col(a["k_k"][0]), col(a["k_a"][0]), col(a["r_k"][0]), col(a["ln_w"][0]),
                         col(a["ln_b"][0])], axis=2).reshape(P, CT * NPC)
    eps = np.tile(np.array([[RMS_EPS, GN_EPS, KK_EPS, 0.0]], np.float32), (P, 1))
    params = np.concatenate([col(a["mu_prev"][0]), col(a["mu_next"][0]), col(a["b_gate"][0]),
                             col(a["norm_pre_mix"][0]), col(a["norm_pre_ffn"][0]), per_pair, eps], axis=1)
    w2, a2, g2 = (a[n][0].reshape(P, CT, P).transpose(1, 0, 2) for n in ("w2", "a2", "g2"))
    win_t = slabs(w_in)
    w_v = rows(w_in[:, 1024:1536]).reshape(P, KD, 2, 256).transpose(2, 0, 1, 3).reshape(2, P, 2 * D)
    rp = np.zeros((8, 2 * WIN_H - 1, 2 * GRID_W - 1), np.float32)
    rp[:, :, GRID_W - WIN_W:GRID_W + WIN_W - 1] = a["rpb"][0]
    cn, cs, cm = host_constants()
    return {
        "x": np.concatenate([a["x_prompt"][0], a["x_sample"][0]], axis=0),
        "w_in": win_t, "w_v": w_v,
        "w_proj": np.concatenate([slabs(a["w_proj_a"][0]), slabs(a["w_proj_b"][0])], axis=2),
        "lora": np.stack([w2, a2, g2], axis=2), "params": params,
        "w_out": rows(a["w_out"][0]), "w_up": slabs(a["w_up"][0]),
        "w_down": a["w_down"][0].reshape(DFF // P, P, D),
        "gains": np.stack([a["norm_post_mix"][0], a["norm_post_ffn"][0]]),
        "rpb": rp, "cn": cn, "cs": cs, "cm": cm,
    }


def kernel(**inputs):
    import numpy as np
    from concourse import bacc
    from concourse.bass_utils import run_bass_kernel_spmd

    laid = {n: np.ascontiguousarray(v) for n, v in
            host_layout({n: np.asarray(v) for n, v in inputs.items()}).items()}
    nc = bacc.Bacc("TRN2", target_bir_lowering=False, num_devices=1)
    args = {n: nc.dram_tensor(f"in_{n}", v.shape, mybir.dt.from_np(v.dtype), kind="ExternalInput").ap()
            for n, v in laid.items()}
    out = nc.dram_tensor("out", [T, D], F32, kind="ExternalOutput").ap()
    encoder(nc, args, out)
    got = run_bass_kernel_spmd(nc, [{f"in_{n}": v for n, v in laid.items()}], core_ids=[0]).results[0]["out"]
    return got[None, 0:TP], got[None, TP:T]
```
